# Optimizing a Trainium2 kernel written in Bass

```python
import math
import jax, jax.numpy as jnp
from jax import lax
import numpy as np

D_MODEL = 1024
BATCH = 1
SEQ = 512
DEPTH = 2
DEC_BATCH = 1
DEC_SEQ = 32
PAST_LEN = 1024

CHUNK = 64
KEY_BLOCK = 16
N_AB = (DEPTH + 1) // 2
N_C = DEPTH // 2
D_A = D_MODEL
P_A = 64
H_A = D_A // P_A
N_A = 128
G_A = 2
CONV_K = 4
CONV_DIM_A = D_A + 2 * G_A * N_A
H_B = 4
DK_B = D_MODEL // 2 // H_B
DV_B = D_MODEL // H_B
GLA_LOWRANK = 16
GLA_GATE_NORM = 16.0
HGRN_EXPAND = 128
H_C = D_MODEL // HGRN_EXPAND
DK_C = HGRN_EXPAND
DV_C = D_MODEL // H_C
D_C = H_C * DK_C
D_FF = 2816
EPS = 1e-6
TINY = 1e-30
IN_AB = D_A + CONV_DIM_A + H_A + 2 * H_B * DK_B + 2 * H_B * DV_B + GLA_LOWRANK
IN_C = 2 * D_C + 2 * H_C * DV_C
F32 = jnp.float32

kernel_name = 'hybrid_ssd_gla_hgrn2_macaron_stream'

def pad_time(a, tp):
    return jnp.pad(a, [(0, 0), (0, tp - a.shape[1])] + [(0, 0)] * (a.ndim - 2))

def blocks(a, size):
    bsz, tp = a.shape[0], a.shape[1]
    return jnp.moveaxis(a.reshape((bsz, tp // size, size) + a.shape[2:]), 1, 0)

def unblocks(a):
    a = jnp.moveaxis(a, 0, 1)
    return a.reshape((a.shape[0], a.shape[1] * a.shape[2]) + a.shape[3:])

def split_cols(a, sizes):
    return jnp.split(a, np.cumsum(sizes)[:-1].tolist(), axis=-1)

def masked_decay(diff, mask):
    return jnp.where(mask, jnp.exp(jnp.where(mask, diff, 0.0)), 0.0)

def rms_norm(x, w):
    xf = x.astype(F32)
    y = xf * lax.rsqrt(jnp.mean(xf * xf, axis=-1, keepdims=True) + EPS)
    return (y * w.astype(F32)).astype(x.dtype)

def swiglu(x, w_gu, w_down):
    gate, up = jnp.split(x @ w_gu, 2, axis=-1)
    return (jax.nn.silu(gate) * up) @ w_down

def causal_dwconv(u, buf, w, b):
    ext = jnp.concatenate([buf.astype(u.dtype), u], axis=1)
    out = lax.conv_general_dilated(ext, w[:, None, :].astype(u.dtype), (1,), 'VALID',
                                   dimension_numbers=('NWC', 'WIO', 'NWC'),
                                   feature_group_count=u.shape[-1])
    return out + b, ext[:, -(CONV_K - 1):]

def ssd_scan(x, dt, a, bm, cm, h0):
    bsz, t, nh, hp = x.shape
    ng, ns = bm.shape[2], bm.shape[3]
    hpg = nh // ng
    tp = -(-t // CHUNK) * CHUNK
    xs = (blocks(pad_time(x, tp).reshape(bsz, tp, ng, hpg, hp), CHUNK),
          blocks(pad_time(dt, tp).reshape(bsz, tp, ng, hpg), CHUNK),
          blocks(pad_time(bm, tp), CHUNK),
          blocks(pad_time(cm, tp), CHUNK))
    a = a.reshape(ng, hpg)
    mask = jnp.tril(jnp.ones((CHUNK, CHUNK), dtype=bool))[None, :, :, None, None]

    def step(h, blk):
        xb, dtb, bb, cb = blk
        cum = jnp.cumsum(dtb * a, axis=1)
        decay = masked_decay(cum[:, :, None] - cum[:, None, :], mask)
        xdt = xb * dtb[..., None]
        cbs = jnp.einsum('bign,bjgn->bijg', cb, bb)
        y = jnp.einsum('bijg,bijgh,bjghp->bighp', cbs, decay, xdt)
        y = y + jnp.einsum('bign,bghpn,bigh->bighp', cb, h, jnp.exp(cum))
        h_new = (h * jnp.exp(cum[:, -1])[..., None, None]
                 + jnp.einsum('bjgn,bjgh,bjghp->bghpn', bb, jnp.exp(cum[:, -1:] - cum), xdt))
        return h_new, y

    h_t, ys = lax.scan(step, h0.reshape(bsz, ng, hpg, hp, ns), xs)
    return unblocks(ys).reshape(bsz, tp, nh, hp)[:, :t], h_t.reshape(bsz, nh, hp, ns)

def gated_la_scan(q, k, v, log_g, s0):
    t = q.shape[1]
    tp = -(-t // KEY_BLOCK) * KEY_BLOCK
    xs = tuple(blocks(pad_time(a, tp), KEY_BLOCK) for a in (q, k, v, log_g))
    mask = jnp.tril(jnp.ones((KEY_BLOCK, KEY_BLOCK), dtype=bool))[None, :, :, None, None]

    def step(s, blk):
        qb, kb, vb, gb = blk
        b = jnp.cumsum(gb, axis=1)
        decay = masked_decay(b[:, :, None] - b[:, None, :], mask)
        att = jnp.einsum('bihk,bijhk,bjhk->bijh', qb, decay, kb)
        o = (jnp.einsum('bijh,bjhv->bihv', att, vb)
             + jnp.einsum('bihk,bhkv->bihv', qb * jnp.exp(b), s))
        b_end = b[:, -1]
        s_new = (s * jnp.exp(b_end)[..., None]
                 + jnp.einsum('bjhk,bjhv->bhkv', kb * jnp.exp(b_end[:, None] - b), vb))
        return s_new, o

    s_t, outs = lax.scan(step, s0, xs)
    return unblocks(outs)[:, :t], s_t

def mixer_ab(u, ssm_h, conv_buf, gla_s, p, j):
    bsz, t, _ = u.shape
    z, xbc, dt, q, k, v, g, glr = split_cols(
        u @ p['ab_w_in'][j],
        [D_A, CONV_DIM_A, H_A, H_B * DK_B, H_B * DK_B, H_B * DV_B, H_B * DV_B, GLA_LOWRANK])
    xbc, conv_new = causal_dwconv(xbc, conv_buf, p['ssm_conv_w'][j], p['ssm_conv_b'][j])
    xbc = jax.nn.silu(xbc).astype(F32)
    xs, bm, cm = split_cols(xbc, [D_A, G_A * N_A, G_A * N_A])
    xs = xs.reshape(bsz, t, H_A, P_A)
    dt = jax.nn.softplus(dt.astype(F32) + p['ssm_dt_bias'][j])
    a = -jnp.exp(p['ssm_a_log'][j].astype(F32))
    y, ssm_new = ssd_scan(xs, dt, a, bm.reshape(bsz, t, G_A, N_A), cm.reshape(bsz, t, G_A, N_A),
                          ssm_h.astype(F32))
    y = (y + p['ssm_d'][j][:, None] * xs).reshape(bsz, t, D_A) * jax.nn.silu(z.astype(F32))
    y = rms_norm(y.reshape(bsz, t, G_A, D_A // G_A),
                 p['ssm_norm_w'][j].reshape(G_A, D_A // G_A)).reshape(bsz, t, D_A)
    q = q.astype(F32).reshape(bsz, t, H_B, DK_B) * DK_B ** -0.5
    k = k.astype(F32).reshape(bsz, t, H_B, DK_B)
    v = v.astype(F32).reshape(bsz, t, H_B, DV_B)
    gk = jax.nn.log_sigmoid((glr @ p['gla_w_gk'][j] + p['gla_b_gk'][j]).astype(F32)) / GLA_GATE_NORM
    o, gla_new = gated_la_scan(q, k, v, gk.reshape(bsz, t, H_B, DK_B), gla_s.astype(F32))
    o = rms_norm(o, p['gla_norm_w'][j]).reshape(bsz, t, H_B * DV_B) * jax.nn.silu(g.astype(F32))
    out = jnp.concatenate([y, o], axis=-1).astype(u.dtype) @ p['ab_w_out'][j]
    return out, ssm_new.astype(ssm_h.dtype), conv_new, gla_new.astype(gla_s.dtype)

def hgrn_lower_bounds(logits):
    s = jax.nn.softmax(logits.astype(F32), axis=0)
    return jnp.cumsum(s, axis=0) - s[0]

def mixer_c(u, s0, p, j, lb):
    bsz, t, _ = u.shape
    q, f, i, g = split_cols(u @ p['c_w_in'][j], [D_C, D_C, H_C * DV_C, H_C * DV_C])
    f = f.astype(F32)
    sig = jax.nn.sigmoid(f)
    forget = lb + (1.0 - lb) * sig
    log_f = jnp.log(jnp.maximum(forget, TINY))
    k = 1.0 - forget
    q = jax.nn.silu(q.astype(F32))
    o, s_new = gated_la_scan(q.reshape(bsz, t, H_C, DK_C), k.reshape(bsz, t, H_C, DK_C),
                             i.astype(F32).reshape(bsz, t, H_C, DV_C),
                             log_f.reshape(bsz, t, H_C, DK_C), s0.astype(F32))
    o = rms_norm(o, p['hgrn_norm_w'][j]).reshape(bsz, t, H_C * DV_C) * jax.nn.silu(g.astype(F32))
    return o.astype(u.dtype) @ p['c_w_out'][j], s_new.astype(s0.dtype)

def trunk(x, ssm0, conv0, gla0, hgrn0, p):
    lbs = hgrn_lower_bounds(p['hgrn_lb_logits'])
    new_ssm, new_conv, new_gla, new_hgrn = [], [], [], []
    h = x
    for l in range(DEPTH):
        h = h + 0.5 * swiglu(rms_norm(h, p['norm_ffn1'][l]), p['ffn1_w_gu'][l], p['ffn1_w_down'][l])
        u = rms_norm(h, p['norm_mix'][l])
        j = l // 2
        if l % 2 == 0:
            m, s_ssm, s_conv, s_gla = mixer_ab(u, ssm0[j], conv0[j], gla0[j], p, j)
            new_ssm.append(s_ssm)
            new_conv.append(s_conv)
            new_gla.append(s_gla)
        else:
            m, s_h = mixer_c(u, hgrn0[j], p, j, lbs[j])
            new_hgrn.append(s_h)
        h = h + m
        h = h + 0.5 * swiglu(rms_norm(h, p['norm_ffn2'][l]), p['ffn2_w_gu'][l], p['ffn2_w_down'][l])
    y = rms_norm(h, p['norm_final'])
    return y, jnp.stack(new_ssm), jnp.stack(new_conv), jnp.stack(new_gla), jnp.stack(new_hgrn)

def setup_inputs(seed: int = 0) -> dict:
    key = jax.random.key(seed)
    keys = list(jax.random.split(key, 40))

    def nrm(shape, scale):
        return scale * jax.random.normal(keys.pop(), shape, F32)

    def gain(shape):
        return 1.0 + 0.02 * jax.random.normal(keys.pop(), shape, F32)

    dt0 = jnp.exp(jax.random.uniform(keys.pop(), (N_AB, H_A), F32, math.log(1e-3), math.log(1e-1)))
    a_log = jnp.log(jax.random.uniform(keys.pop(), (N_AB, H_A), F32, 1.0, 16.0))
    w_out_ab = D_A + H_B * DV_B
    return {
        'x_prompt': nrm((BATCH, SEQ, D_MODEL), 1.0),
        'x_sample': nrm((DEC_BATCH, DEC_SEQ, D_MODEL), 1.0),
        'state_ssm': nrm((N_AB, DEC_BATCH, H_A, P_A, N_A), 0.05),
        'state_conv': nrm((N_AB, DEC_BATCH, CONV_K - 1, CONV_DIM_A), 1.0),
        'state_gla': nrm((N_AB, DEC_BATCH, H_B, DK_B, DV_B), 0.5),
        'state_hgrn': nrm((N_C, DEC_BATCH, H_C, DK_C, DV_C), 0.5),
        'norm_ffn1': gain((DEPTH, D_MODEL)),
        'ffn1_w_gu': nrm((DEPTH, D_MODEL, 2 * D_FF), D_MODEL ** -0.5),
        'ffn1_w_down': nrm((DEPTH, D_FF, D_MODEL), D_FF ** -0.5),
        'norm_mix': gain((DEPTH, D_MODEL)),
        'ab_w_in': nrm((N_AB, D_MODEL, IN_AB), D_MODEL ** -0.5),
        'ssm_conv_w': nrm((N_AB, CONV_K, CONV_DIM_A), CONV_K ** -0.5),
        'ssm_conv_b': nrm((N_AB, CONV_DIM_A), 0.02),
        'ssm_dt_bias': dt0 + jnp.log(-jnp.expm1(-dt0)),
        'ssm_a_log': a_log,
        'ssm_d': gain((N_AB, H_A)),
        'ssm_norm_w': gain((N_AB, D_A)),
        'gla_w_gk': nrm((N_AB, GLA_LOWRANK, H_B * DK_B), GLA_LOWRANK ** -0.5),
        'gla_b_gk': nrm((N_AB, H_B * DK_B), 0.02),
        'gla_norm_w': gain((N_AB, DV_B)),
        'ab_w_out': nrm((N_AB, w_out_ab, D_MODEL), w_out_ab ** -0.5),
        'c_w_in': nrm((N_C, D_MODEL, IN_C), D_MODEL ** -0.5),
        'hgrn_lb_logits': nrm((N_C, D_C), 1.0),
        'hgrn_norm_w': gain((N_C, DV_C)),
        'c_w_out': nrm((N_C, H_C * DV_C, D_MODEL), (H_C * DV_C) ** -0.5),
        'norm_ffn2': gain((DEPTH, D_MODEL)),
        'ffn2_w_gu': nrm((DEPTH, D_MODEL, 2 * D_FF), D_MODEL ** -0.5),
        'ffn2_w_down': nrm((DEPTH, D_FF, D_MODEL), D_FF ** -0.5),
        'norm_final': gain((D_MODEL,)),
    }

def reference(x_prompt, x_sample, state_ssm, state_conv, state_gla, state_hgrn,
              norm_ffn1, ffn1_w_gu, ffn1_w_down, norm_mix, ab_w_in, ssm_conv_w, ssm_conv_b,
              ssm_dt_bias, ssm_a_log, ssm_d, ssm_norm_w, gla_w_gk, gla_b_gk, gla_norm_w, ab_w_out,
              c_w_in, hgrn_lb_logits, hgrn_norm_w, c_w_out, norm_ffn2, ffn2_w_gu, ffn2_w_down,
              norm_final):
    p = dict(norm_ffn1=norm_ffn1, ffn1_w_gu=ffn1_w_gu, ffn1_w_down=ffn1_w_down, norm_mix=norm_mix,
             ab_w_in=ab_w_in, ssm_conv_w=ssm_conv_w, ssm_conv_b=ssm_conv_b, ssm_dt_bias=ssm_dt_bias,
             ssm_a_log=ssm_a_log, ssm_d=ssm_d, ssm_norm_w=ssm_norm_w, gla_w_gk=gla_w_gk,
             gla_b_gk=gla_b_gk, gla_norm_w=gla_norm_w, ab_w_out=ab_w_out, c_w_in=c_w_in,
             hgrn_lb_logits=hgrn_lb_logits, hgrn_norm_w=hgrn_norm_w, c_w_out=c_w_out,
             norm_ffn2=norm_ffn2, ffn2_w_gu=ffn2_w_gu, ffn2_w_down=ffn2_w_down, norm_final=norm_final)
    bp = x_prompt.shape[0]
    dtp = x_prompt.dtype
    y_prompt, ssm_p, conv_p, gla_p, hgrn_p = trunk(
        x_prompt,
        jnp.zeros((N_AB, bp, H_A, P_A, N_A), dtp),
        jnp.zeros((N_AB, bp, CONV_K - 1, CONV_DIM_A), dtp),
        jnp.zeros((N_AB, bp, H_B, DK_B, DV_B), dtp),
        jnp.zeros((N_C, bp, H_C, DK_C, DV_C), dtp),
        p)
    y_sample, ssm_s, conv_s, gla_s, hgrn_s = trunk(x_sample, state_ssm, state_conv, state_gla,
                                                   state_hgrn, p)
    return (y_prompt, y_sample, ssm_p, conv_p, gla_p, hgrn_p, ssm_s, conv_s, gla_s, hgrn_s)


_drawn_inputs = setup_inputs


def setup_inputs(seed=0):
    import zlib

    import numpy as np

    out = dict(_drawn_inputs(seed))
    spreads = {}
    factors = {'state_hgrn': 4.603,
     'norm_ffn1': 3.721,
     'ssm_d': 16.286,
     'ssm_norm_w': 15.265,
     'gla_b_gk': 6.607,
     'gla_norm_w': 22.645,
     'hgrn_norm_w': 54.072,
     'norm_ffn2': 6.143,
     'norm_final': 7.936}
    for name, (base, spread) in spreads.items():
        noise = np.random.default_rng([zlib.crc32(name.encode()), seed]).standard_normal(out[name].shape)
        drawn = base * np.exp(spread * noise) if base else spread * noise
        out[name] = __import__('jax').numpy.asarray(drawn.astype(out[name].dtype))
    for name, factor in factors.items():
        out[name] = (out[name] * factor).astype(out[name].dtype)
    return out
```

```python
from contextlib import ExitStack

import concourse.bass as bass
from concourse import mybir

F = mybir.dt.float32
FR = mybir.dt.float32r
I32 = mybir.dt.int32
ALU = mybir.AluOpType
ACT = mybir.ActivationFunctionType
ds = bass.ds

P = 128
D = 1024
KT = D // P
TP, TS = 512, 32
T = TP + TS
HT = T // 2
CH = 128
NC = TP // CH
TPAD = TP + CH
FF = 2816
FT = FF // P
GROUPS = [(0, 12), (12, 10)]
NXT = 12
HA, PA = 16, 64
COL_Z, COL_XBC, COL_DT, COL_Q, COL_K, COL_V, COL_G, COL_LR = 0, 1024, 2560, 2576, 3088, 3600, 4624, 5648
EPS = 1e-6
TINY = 1e-30
CREDIT = 4
TREE = [64, 32, 16, 8, 4, 2, 1]
LV = len(TREE) + 1
V_F1, V_MIX, V_F2, V_FIN, V_CW, V_CB, V_SN = 0, 16, 32, 48, 56, 104, 116
V_GN, V_HN, V_BG, V_LB = 128, 130, 131, 135
NV = 143
NORM_COL = [V_F1, V_MIX, V_F2, V_F1 + 8, V_MIX + 8, V_F2 + 8, V_FIN]


def dense_plan():
    phases, rows = [], []

    def phase(name, n, k):
        phases.append((name, len(rows), n, k))
        rows.extend([k] * n)

    def ffn(tag):
        for g, (_, nf) in enumerate(GROUPS):
            phase(f"{tag}_up{g}", 2 * nf, KT)
            phase(f"{tag}_down{g}", KT, nf)

    ffn("l0f1")
    phase("ab_small", 1, KT)
    phase("ab_xbc", NXT, KT)
    phase("ab_z", KT, KT)
    phase("ab_outy", KT, KT)
    phase("ab_heads", 16, KT)
    phase("ab_g", KT, KT)
    phase("ab_outo", KT, KT)
    ffn("l0f2")
    ffn("l1f1")
    phase("c_heads", 32, KT)
    phase("c_out", KT, KT)
    ffn("l1f2")
    return phases, rows


def build(nc, a, o):
    phases, unit_rows = dense_plan()
    plan = {name: (u, n, k) for name, u, n, k in phases}

    with ExitStack() as ctx:
        def sem(name):
            return ctx.enter_context(nc.semaphore(name))

        def at(name, shape, offset, dt=F):
            return nc.alloc_sbuf_tensor_at(name, [P] + list(shape), dt, offset=offset)

        def place(name, shape, where, dt=F):
            off, n = where[0], 4
            for s in shape:
                n *= s
            where[0] += (n + 63) // 64 * 64
            assert where[0] <= nc.sbuf_usable_end, (name, where[0], nc.sbuf_usable_end)
            return at(name, shape, off, dt)

        w = [(nc.sbuf_base + 63) // 64 * 64]
        H = place("H", [KT, T], w)
        XH = place("XH", [KT, T], w, FR)
        XL = place("XL", [KT, T], w, FR)
        raw = [place(f"raw{s}", [12, P], w) for s in range(4)]
        whi = [place(f"whi{s}", [12, P], w, FR) for s in range(2)]
        wlo = [place(f"wlo{s}", [12, P], w, FR) for s in range(2)]
        RS = place("RS", [T], w)
        LR = place("LR", [T], w)
        SQ = place("SQ", [T], w)
        ACC = place("ACC", [T], w)
        ident = place("ident", [P], w)
        ones = place("ones", [P], w)
        vec = place("vec", [NV], w)
        cst = place("cst", [36], w)
        LB = place("LB", [4, KT], w)
        eps = place("eps", [1], w)
        free = w[0]

        w = [free]
        xin = place("xin", [NC + 1, D], w)
        rows = place("rows", [3, P], w)
        w = [free]
        YF = place("YF", [KT, TPAD], w)
        yout = place("yout", [2, D], w)
        w = [free]
        AH = place("AH", [12, T], w, FR)
        AL = place("AL", [12, T], w, FR)
        TG = place("TG", [T], w)
        TU = place("TU", [T], w)
        AV = place("AV", [T], w)
        w = [free]
        TRI = place("TRI", [P], w)
        DTG = place("DTG", [T], w)
        WGK = place("WGK", [512], w)
        keep_ab = w[0]
        XC = place("XC", [NXT, T], w)
        YH = at("YH", [KT, T], keep_ab, FR)
        keep_sz = w[0]
        SZ = place("SZ", [KT, T], w)
        YL = at("YL", [KT, T], keep_sz, FR)
        ssd0 = w[0]
        XE = [place(f"XE{b}", [T + 6], w) for b in range(2)]
        CV = [place(f"CV{b}", [T + 3], w) for b in range(2)]
        XLAST = place("XLAST", [P], w)
        CLST = place("CLST", [P], w)
        DTW = place("DTW", [8, T], w)
        w = [ssd0]
        DC = LR
        XCC = place("XCC", [NXT, CH], w)
        DCC = place("DCC", [CH], w)
        DCT = place("DCT", [P], w)
        CE = place("CE", [HA], w)
        EE = place("EE", [HA], w)
        DE = place("DE", [HA], w)
        HIO = at("HIO", [KT, P], w[0])
        XD = place("XD", [D], w)
        XDE = place("XDE", [D], w)
        BT = place("BT", [2 * P], w)
        CBM = place("CBM", [2, CH], w)
        LM = place("LM", [4, 4, CH], w)
        EP = place("EP", [KT, CH], w)
        Y = place("Y", [KT, CH], w)
        RY = place("RY", [2, CH], w)
        HS = place("HS", [D], w)
        DCOL = place("DCOL", [KT], w)
        D16 = place("D16", [1], w)
        SEL = place("SEL", [HA, P], w)
        SELP = place("SELP", [KT, P], w)

        def scan_memory(tag, start, nv):
            w = [start]
            m = {n: place(tag + n, s, w) for n, s in dict(
                st=[4, T], qw=[T], kw=[T], gw=[T], vw=[nv, TPAD], gs=[T], bw=[T], e1=[T], qe=[T], kd=[TPAD],
                xl=[LV - 1, T], vt=[NC + 1, nv * P], kt=[NC + 1, P], att=[NC, CH], ats=[TS], s=[NC + 1, nv * P],
                si=[nv * P], et=[NC + 1], rm=[T], mask=[5, P], wg=[P], o=[nv, T], sq=[nv, T]).items()}
            m["end"], m["nv"] = w[0], nv
            m["rh"], m["gn"] = LR, SQ
            return m

        GM = scan_memory("g_", keep_ab, 2)
        w = [GM["end"]]
        ON = place("ON", [KT, T], w)
        w = [keep_ab]
        GOH = place("GOH", [KT, T], w, FR)
        GOL = place("GOL", [KT, T], w, FR)
        GG = place("GG", [T], w)
        GS = place("GS", [T], w)
        assert w[0] <= GM["end"]
        CM = scan_memory("c_", free, 1)
        w = [CM["end"]]
        COH = place("COH", [KT, T], w, FR)
        COL = place("COL", [KT, T], w, FR)

        PD = ctx.enter_context(nc.psum_tensor("PD", [P, 4, 512], F))
        PM = ctx.enter_context(nc.psum_tensor("PM", [P, 4, 512], F))

        def pair(b):
            return PD[:, 2 * (b % 2):2 * (b % 2) + 2, 0:HT]

        def two(x):
            return x.rearrange("p (s t) -> p s t", s=2)

        def tile(x, m):
            return x[:, ds(m, 1), :].rearrange("p a t -> p (a t)")

        names = """hi_ready lo_ready unit_done pair_read consts_made rows_landed vec_psum vec_ready x_psum h_ready
            xh_ready xl_ready sq_ready acc_done ms_ready rs_ready gate_scaled silu_done act_made ah_ready al_ready
            lowrank_landed lb_in lb_exp small_landed ab_masks conv_ready xc_ready z_scaled sz_ready
            dt_abs dt_exp dt_plus dt_log last_rows last_psum last_copied last_stored d_landed d_psum selectors
            ssd_ready chunk_copied chunk_turned chunk_dct end_psum end_diff end_exp x_scaled cb_psum cb_masked
            cum_psum cum_diff decay_exp decay_made spread_psum spread_exp y_psum y_gated y_squared y_mean y_rstd
            y_weighted yh_ready yl_ready state_psum state_new h0_psum h0_landed h0_ready hout_psum hout_copied
            hout_stored scan_consts_made st_ready gn_ready wg_copied gk_psum pre_act forget_made logs_made b_ready e1_ready
            kd_diff kd_exp kd_ready tree_diff tree_exp tree_made turned turned_read level_psum level_placed
            kv_psum s_ready o_psum o_copied o_mean o_rstd o_scaled oh_ready head_out s0_landed sp_stored ss_stored
            g_scaled gs_ready go_made goh_ready gol_ready y_ready yt_psum yt_copied yc_read""".split()
        S = {n: sem(n) for n in names}
        raw_landed = [sem(f"raw_landed{s}") for s in range(4)]
        x_landed = [sem(f"x_landed{s}") for s in range(2)]
        y_stored = [sem(f"y_stored{s}") for s in range(2)]
        passed = {e: sem(f"waits_passed_{e}") for e in ("sp", "act", "dve", "pe", "pool")}
        engines = {"sp": nc.sync, "act": nc.scalar, "dve": nc.vector, "pe": nc.tensor, "pool": nc.gpsimd}

        def hold(e, s, value):
            engines[e].wait_ge(s, value)
            if not isinstance(value, int):
                engines[e].sem_inc(passed[e], 1)

        def loop(e, lo, hi, body):
            if hi - lo >= 2:
                with engines[e].Fori(lo, hi) as i:
                    body(i)
            elif hi - lo == 1:
                body(lo)

        block = ctx.enter_context(nc.Block())

        @block.sync
        def _(sp):
            sp.wait_ge(S["consts_made"], 1)
            for col, name, pat, n in [
                    (V_F1, "norm_ffn1", "l (c p) -> (l c) p", 16), (V_MIX, "norm_mix", "l (c p) -> (l c) p", 16),
                    (V_F2, "norm_ffn2", "l (c p) -> (l c) p", 16), (V_FIN, "norm_final", "(c p) -> c p", 8),
                    (V_CW, "ssm_conv_w", "o k (c p) -> (o k c) p", 48), (V_CB, "ssm_conv_b", "o (c p) -> (o c) p", 12),
                    (V_SN, "ssm_norm_w", "o (c p) -> (o c) p", 8), (V_GN, "gla_norm_w", "o (c p) -> (o c) p", 2),
                    (V_HN, "hgrn_norm_w", "o (c p) -> (o c) p", 1), (V_BG, "gla_b_gk", "o (c p) -> (o c) p", 4),
                    (V_LB, "hgrn_lb_logits", "o (c p) -> (o c) p", 8), (2 * P, "state_conv", "o b r (c p) -> (o b r c) p", 36)]:
                sp.dma_start(rows[col % P:col % P + n, col // P, :], a[name].rearrange(pat, p=P)).then_inc(S["rows_landed"], 16)
            sp.dma_start(xin[:, 0:NC, :], a["x_prompt"].rearrange("b (c t) d -> t (b c) d", t=CH)).then_inc(x_landed[0], 16)
            sp.dma_start(xin[0:TS, NC, :], a["x_sample"].rearrange("b t d -> (b t) d")).then_inc(x_landed[1], 16)

            def load(u, slot, src, k, n=P, dst=0):
                hold("sp", S["lo_ready"], u + 1)
                return sp.dma_start(raw[slot][:, 0:k, dst:dst + n], src)

            def columns(name, view, start=0, end=None):
                u0, n, k = plan[name]

                def body(i):
                    for b in range(4):
                        s = (u0 + b) % 4
                        load(u0 + 4 * i + b, s, view(b, i), k).then_inc(raw_landed[s], 16)
                loop("sp", start, n // 4 if end is None else end, body)

            def ffn(tag, gu, down):
                gu = gu.rearrange("(k p) n -> p k n", p=P)
                for g, (f0, nf) in enumerate(GROUPS):
                    columns(f"{tag}_up{g}", lambda b, i: gu[:, :, ds(i * (2 * P) + ((b % 2) * FF + (f0 + b // 2) * P), P)])
                    dn = down[f0 * P:(f0 + nf) * P, :].rearrange("(k p) n -> p k n", p=P)
                    columns(f"{tag}_down{g}", lambda b, i: dn[:, :, ds(i * (4 * P) + b * P, P)])

            def plain(w, col):
                return lambda b, i: w[:, :, ds(i * (4 * P) + (col + b * P), P)]

            win = a["ab_w_in"][0].rearrange("(k p) n -> p k n", p=P)
            wy = a["ab_w_out"][0][0:D, :].rearrange("(k p) n -> p k n", p=P)
            wo = a["ab_w_out"][0][D:2 * D, :].rearrange("(k p) n -> p k n", p=P)
            cin = a["c_w_in"][0].rearrange("(k p) n -> p k n", p=P)
            cout = a["c_w_out"][0].rearrange("(k p) n -> p k n", p=P)

            ffn("l0f1", a["ffn1_w_gu"][0], a["ffn1_w_down"][0])
            u = plan["ab_small"][0]
            load(u, u % 4, win[:, :, COL_DT:COL_DT + HA], KT, HA, 0).then_inc(raw_landed[u % 4], 16)
            load(u, u % 4, win[:, :, COL_LR:COL_LR + 16], KT, 16, 32).then_inc(S["lowrank_landed"], 16)
            sp.wait_ge(S["h_ready"], 2 * KT)
            sp.dma_start(WGK[32:48, :], a["gla_w_gk"][0]).then_inc(S["small_landed"], 16)
            sp.dma_start(DTW[0:HA, 7, 0:1], a["ssm_dt_bias"].rearrange("o h -> h o")).then_inc(S["small_landed"], 16)
            sp.dma_start(DTW[0:HA, 7, 1:2], a["ssm_a_log"].rearrange("o h -> h o")).then_inc(S["small_landed"], 16)
            columns("ab_xbc", plain(win, COL_XBC))
            columns("ab_z", plain(win, COL_Z))
            columns("ab_outy", plain(wy, 0), 0, 1)
            sp.wait_ge(S["last_copied"], 1)
            sp.dma_start(o["conv_p"].rearrange("o b r (c p) -> (o b r c) p", p=P), CLST[0:36, :]).then_inc(S["last_stored"], 16)
            sp.dma_start(o["conv_s"].rearrange("o b r (c p) -> (o b r c) p", p=P), CLST[36:72, :]).then_inc(S["last_stored"], 16)
            sp.wait_ge(S["last_stored"], 32)
            sp.sem_inc(S["ssd_ready"], 1)
            sp.wait_ge(S["ssd_ready"], 3)
            sp.dma_start(D16[32:48, 0:1], a["ssm_d"].rearrange("o h -> h o")).then_inc(S["d_landed"], 16)
            ssm = "o b (m e) p n -> (e p) (o b m) n"
            sp.wait_ge(S["hout_copied"], 1)
            for e in range(2):
                sp.dma_start(o["ssm_p"].rearrange(ssm, e=2)[e * PA:(e + 1) * PA], HIO[e * PA:(e + 1) * PA, :, :]).then_inc(S["hout_stored"], 16)
            sp.wait_ge(S["hout_stored"], 32)
            for e in range(2):
                sp.dma_start(HIO[e * PA:(e + 1) * PA, :, :], a["state_ssm"].rearrange(ssm, e=2)[e * PA:(e + 1) * PA]).then_inc(S["h0_landed"], 16)
            sp.wait_ge(S["hout_copied"], 2)
            for e in range(2):
                sp.dma_start(o["ssm_s"].rearrange(ssm, e=2)[e * PA:(e + 1) * PA], HIO[e * PA:(e + 1) * PA, :, :]).then_inc(S["hout_stored"], 16)
            sp.wait_ge(S["hout_stored"], 64)
            columns("ab_outy", plain(wy, 0), 1)
            u0 = plan["ab_heads"][0]

            def gla(h):
                for b, col in enumerate([ds(h * P + COL_Q, P), ds(h * P + COL_K, P),
                                         ds(h * (2 * P) + COL_V, P), ds(h * (2 * P) + (COL_V + P), P)]):
                    s = (u0 + b) % 4
                    load(u0 + 4 * h + b, s, win[:, :, col], KT).then_inc(raw_landed[s], 16)
            loop("sp", 0, 4, gla)
            columns("ab_g", plain(win, COL_G))
            columns("ab_outo", plain(wo, 0))
            ffn("l0f2", a["ffn2_w_gu"][0], a["ffn2_w_down"][0])
            ffn("l1f1", a["ffn1_w_gu"][1], a["ffn1_w_down"][1])
            columns("c_heads", lambda b, h: cin[:, :, ds(h * P + b * D, P)])
            columns("c_out", plain(cout, 0))
            ffn("l1f2", a["ffn2_w_gu"][1], a["ffn2_w_down"][1])
            for c in range(NC + 1):
                sp.wait_ge(S["yt_copied"], c + 1)
                dst = o["y_p"][0, c * CH:(c + 1) * CH, :] if c < NC else o["y_s"][0]
                sp.dma_start(dst, yout[0:CH if c < NC else TS, c % 2, :]).then_inc(y_stored[c % 2], 16)
            sp.wait_ge(y_stored[0], 48)
            sp.wait_ge(y_stored[1], 32)
            sp.wait_ge(S["sp_stored"], 16 * 13)
            sp.wait_ge(S["ss_stored"], 16 * 13)

        @block.gpsimd
        def _(pool):
            pool.sem_inc(S["lo_ready"], CREDIT)
            pool.memset(rows[:, :, :], 0.0).then_inc(S["consts_made"], 1)
            pool.memset(ident[:, :], 0.0)
            pool.memset(ones[:, :], 1.0)
            pool.memset(eps[:, :], EPS)
            pool.drain()
            pool.affine_select(out=ident[:, :], in_=ident[:, :], compare_op=ALU.not_equal, fill=1.0, base=0,
                               pattern=[[-1, P]], channel_multiplier=1)
            pool.drain().then_inc(S["consts_made"], 1)

            def ab_masks():
                pool.wait_ge(S["h_ready"], 2 * KT)
                pool.memset(TRI[:, :], 1.0)
                pool.memset(XLAST[:, :], 0.0)
                pool.memset(XE[0][:, 0:3], 0.0)
                pool.memset(XE[1][:, 0:3], 0.0)
                pool.drain()
                pool.affine_select(out=TRI[:, :], in_=TRI[:, :], compare_op=ALU.is_ge, fill=0.0, base=0,
                                   pattern=[[1, P]], channel_multiplier=-1)
                pool.drain().then_inc(S["ab_masks"], 1)

            def selectors():
                pool.wait_ge(S["ssd_ready"], 3)
                pool.memset(SEL[:, :, :], 0.0)
                pool.memset(SELP[:, :, :], 0.0)
                pool.memset(HS[:, :], 0.0)
                pool.drain()
                pool.affine_select(out=SEL[:, :, :], in_=SEL[:, :, :], compare_op=ALU.not_equal, fill=1.0,
                                   base=-32, pattern=[[-1, HA], [0, P]], channel_multiplier=1)
                halves = SELP[:, :, :].rearrange("p m (e q) -> p m e q", e=2)
                pool.affine_select(out=halves, in_=halves, compare_op=ALU.not_equal, fill=1.0,
                                   base=-32, pattern=[[-2, KT], [-1, 2], [0, PA]], channel_multiplier=1)
                pool.drain().then_inc(S["selectors"], 1)

            def scan_consts(m):
                pool.memset(m["rm"][:, :], 1.0)
                pool.memset(m["mask"][:, :, :], 0.0)
                pool.memset(m["att"][:, :, :], 0.0)
                pool.memset(m["ats"][:, :], 0.0)
                pool.memset(m["vw"][:, :, T:TPAD], 0.0)
                pool.memset(m["kd"][:, T:TPAD], 0.0)
                pool.drain()
                pool.memset(m["rm"][:, 0:T:CH], 0.0)
                for n, hf in enumerate(TREE[2:]):
                    nodes = P // (2 * hf)
                    right = m["mask"][:, n, :].rearrange("p (b s r) -> p b s r", s=2, r=hf)[:, :, 1, :]
                    pool.memset(right, 1.0)
                    pool.drain()
                    pool.affine_select(out=right, in_=right, compare_op=ALU.is_ge, fill=0.0, base=0,
                                       pattern=[[-2 * hf, nodes], [0, hf]], channel_multiplier=1)
                    pool.drain()
                    pool.affine_select(out=right, in_=right, compare_op=ALU.is_ge, fill=0.0, base=hf - 1,
                                       pattern=[[2 * hf, nodes], [0, hf]], channel_multiplier=-1)
                pool.drain().then_inc(S["scan_consts_made"], 1)

            for name, u0, n, k in phases:
                if name == "ab_small":
                    ab_masks()
                if name == "ab_outy":
                    selectors()
                if name == "ab_heads":
                    pool.wait_ge(S["unit_done"], u0 + CREDIT)
                    scan_consts(GM)
                if name == "c_heads":
                    pool.wait_ge(S["h_ready"], 5 * KT)
                    scan_consts(CM)

                def body(i):
                    for b in range(min(4, n)):
                        hold("pool", S["hi_ready"], u0 + 4 * i + (b + 1))
                        pool.tensor_tensor(wlo[(u0 + b) % 2][:, 0:k, :], raw[(u0 + b) % 4][:, 0:k, :],
                                           whi[(u0 + b) % 2][:, 0:k, :].bitcast(F), ALU.subtract).then_inc(S["lo_ready"], 1)
                loop("pool", 0, max(n // 4, 1), body)

        @block.scalar
        def _(act):
            A = act.activation

            def hi(ps, i, k):
                hold("act", raw_landed[ps % 4], 16 * i + 16 * (ps // 4 + 1))
                if ps == plan["ab_small"][0]:
                    act.wait_ge(S["lowrank_landed"], 16)
                hold("act", S["unit_done"], 4 * i + (ps - 1 + CREDIT))
                A(whi[ps % 2][:, 0:k, :], raw[ps % 4][:, 0:k, :], ACT.Copy).then_inc(S["hi_ready"], 1)

            def run(name, evac):
                u0, n, k = plan[name]
                steps = max(n // 4, 1)

                def body(i):
                    for b in range(min(4, n)):
                        hi(u0 + b + 2, i, k)
                        evac(i, b)
                loop("act", 0, steps - 1, body)
                i = steps - 1
                for b in range(min(4, n)):
                    ahead = u0 + 4 * i + b + 2
                    if ahead < len(unit_rows):
                        hi(ahead, 0, unit_rows[ahead])
                    evac(i, b)

            def x_out(e, m, final=False):
                hold("act", S["h_ready"], m + (e * KT + 1))
                if not final:
                    A(tile(XH, m), tile(H, m), ACT.Copy, scale=vec[:, ds(m + NORM_COL[e], 1)]).then_inc(S["xh_ready"], 1)
                hold("act", S["acc_done"], m + (9 * e + 1))
                A(SQ[:, :], tile(H, m), ACT.Square).then_inc(S["sq_ready"], 1)

            def rms(e):
                act.wait_ge(S["ms_ready"], e + 1)
                A(two(LR[:, :]), PM[:, 0:2, 0:HT], ACT.Ln, scale=1.0 / D, bias=eps[:, 0:1])
                act.drain()
                A(RS[:, :], LR[:, :], ACT.Exp, scale=-0.5).then_inc(S["rs_ready"], 1)

            hidden = [0]

            def ffn(tag, e, final=False):
                for g, (f0, nf) in enumerate(GROUPS):
                    base = hidden[0]

                    def up(i, b):
                        if b % 2 == 0:
                            hold("act", S["gate_scaled"], 2 * i + (base + b // 2 + 1))
                            A(TG[:, :], TG[:, :], ACT.Silu).then_inc(S["silu_done"], 1)
                        else:
                            hold("act", S["act_made"], 2 * i + (base + b // 2 + 1))
                            A(tile(AH, 2 * i + b // 2), AV[:, :], ACT.Copy).then_inc(S["ah_ready"], 1)
                    run(f"{tag}_up{g}", up)
                    hidden[0] += nf
                    run(f"{tag}_down{g}", (lambda i, b: x_out(e, 4 * i + b, final)) if g else (lambda i, b: None))
                rms(e)

            act.sem_inc(S["xc_ready"], 2)
            act.wait_ge(S["vec_psum"], 1)
            A(vec[:, 0:P], PM[:, 2, 0:P], ACT.Copy)
            A(vec[:, P:NV], PM[:, 2, P:NV], ACT.Copy)
            A(cst[:, :], PM[:, 2, 2 * P:2 * P + 36], ACT.Copy)
            act.drain().then_inc(S["vec_ready"], 1)
            act.wait_ge(S["lb_in"], 1)
            A(LB[:, 1, :], LB[:, 0, :], ACT.Exp).then_inc(S["lb_exp"], 1)
            for u in range(2):
                act.wait_ge(raw_landed[u], 16)
                A(whi[u][:, 0:KT, :], raw[u][:, 0:KT, :], ACT.Copy).then_inc(S["hi_ready"], 1)
            for m in range(KT):
                x_out(0, m)
            rms(0)
            ffn("l0f1", 1)

            run("ab_small", lambda i, b: None)

            def xbc(i, b):
                hold("act", S["conv_ready"], 4 * i + (b + 1))
                A(XC[:, ds(4 * i + b, 1), 0:TP].rearrange("p a t -> p (a t)"), CV[b % 2][:, 0:TP], ACT.Silu)
                A(XC[:, ds(4 * i + b, 1), TP:T].rearrange("p a t -> p (a t)"), CV[b % 2][:, TP + 3:T + 3], ACT.Silu)
                act.drain().then_inc(S["xc_ready"], 1)
            run("ab_xbc", xbc)

            def z(i, b):
                hold("act", S["z_scaled"], 4 * i + (b + 1))
                A(tile(SZ, 4 * i + b), tile(SZ, 4 * i + b), ACT.Silu).then_inc(S["sz_ready"], 1)
            run("ab_z", z)

            act.wait_ge(S["dt_abs"], 1)
            A(DTW[0:HA, 2, :], DTW[0:HA, 1, :], ACT.Exp, scale=-1.0)
            A(DTW[0:HA, 7, 2:3], DTW[0:HA, 7, 1:2], ACT.Exp)
            act.drain().then_inc(S["dt_exp"], 1)
            act.wait_ge(S["dt_plus"], 1)
            A(DTW[0:HA, 4, :], DTW[0:HA, 3, :], ACT.Ln).then_inc(S["dt_log"], 1)
            act.wait_ge(S["last_psum"], 1)
            A(CLST[:, :], PM[:, 2, 0:P], ACT.Copy).then_inc(S["last_copied"], 1)

            def ssd_chunk(c, t0):
                act.drain()
                hold("act", S["state_new"], c + 1)
                hold("act", S["yl_ready"], c + 1)
                n = CH if not isinstance(c, int) else TS
                A(XCC[:, :, 0:n], XC[:, :, ds(t0, n)], ACT.Copy)
                A(DCC[:, 0:n], DC[:, ds(t0, n)], ACT.Copy)
                act.drain().then_inc(S["chunk_copied"], 1)
                hold("act", S["end_diff"], c + 1)
                A(EE[:, :], EE[:, :], ACT.Exp)
                A(DE[:, :], DE[:, :], ACT.Exp)
                act.drain().then_inc(S["end_exp"], 1)
                for q in range(4):
                    hold("act", S["cum_diff"], 4 * c + (q + 1))
                    A(LM[:, q], LM[:, q], ACT.Exp).then_inc(S["decay_exp"], 1)
                hold("act", S["spread_psum"], c + 1)
                for b in range(2):
                    A(EP[:, 4 * b:4 * b + 4, :].rearrange("p m t -> p (m t)"), PM[:, b, :], ACT.Exp)
                act.drain().then_inc(S["spread_exp"], 1)
                hold("act", S["y_gated"], c + 1)
                A(EP[:, :, :], Y[:, :, :], ACT.Square).then_inc(S["y_squared"], 1)
                hold("act", S["y_mean"], c + 1)
                ry = RY[:, :, :].rearrange("p g t -> p (g t)")
                A(ry, PM[:, 2, 0:2 * CH], ACT.Ln, scale=2.0 / D, bias=eps[:, 0:1])
                act.drain()
                A(ry, ry, ACT.Exp, scale=-0.5).then_inc(S["y_rstd"], 1)
                hold("act", S["y_weighted"], c + 1)
                A(YH[:, :, ds(t0, n)], Y[:, :, 0:n], ACT.Copy).then_inc(S["yh_ready"], 1)

            def state_rows(k):
                act.wait_ge(S["hout_psum"], k)
                for b in range(2):
                    A(HIO[:, 4 * b:4 * b + 4, :].rearrange("p m n -> p (m n)"), PM[:, b, :], ACT.Copy)
                act.drain().then_inc(S["hout_copied"], 1)

            act.wait_ge(S["d_psum"], 1)
            A(DCOL[:, :], PM[:, 3, 0:KT], ACT.Copy).then_inc(S["h0_ready"], 1)
            with act.Fori(0, NC) as c:
                ssd_chunk(c, c * CH)
            state_rows(1)
            act.wait_ge(S["h0_psum"], 1)
            for b in range(2):
                A(HS[:, 512 * b:512 * b + 512], PM[:, 2 + b, :], ACT.Copy)
            act.drain().then_inc(S["h0_ready"], 1)
            ssd_chunk(NC, TP)
            state_rows(2)
            run("ab_outy", lambda i, b: None)

            def heads(name, nh, m, g0, scale, t0):
                u0 = plan[name][0]
                nv = m["nv"]
                gla = nv == 2

                def scan(j):
                    g = j + g0
                    st = m["st"]

                    def load_state():
                        src = (a["state_gla"] if gla else a["state_hgrn"])[0, 0]
                        act.dma_start(m["si"][:, :], src[ds(j, 1), :, :].rearrange("h k v -> k (h v)")).then_inc(S["s0_landed"], 16)

                    def pre():
                        hold("act", S["st_ready"], 4 * g + 3)
                        if gla:
                            A(m["wg"][32:48, :], WGK[32:48, ds(j * P, P)], ACT.Copy).then_inc(S["wg_copied"], 1)
                            A(m["qw"][:, :], st[:, 0, :], ACT.Copy, scale=float(P) ** -0.5)
                            A(m["kw"][:, :], st[:, 1, :], ACT.Copy)
                            hold("act", S["st_ready"], 4 * g + 4)
                            A(m["vw"][:, :, 0:T], st[:, 2:4, :], ACT.Copy)
                            hold("act", S["gk_psum"], g + 1)
                            bias = vec[:, ds(j + V_BG, 1)]
                            A(two(m["gw"][:, :]), PM[:, 0:2, 0:HT], ACT.Identity, bias=bias)
                            A(two(m["e1"][:, :]), PM[:, 0:2, 0:HT], ACT.Abs, bias=bias)
                            act.drain()
                            A(m["e1"][:, :], m["e1"][:, :], ACT.Exp, scale=-1.0)
                            act.drain()
                            A(m["e1"][:, :], m["e1"][:, :], ACT.Ln, bias=1.0)
                            act.drain().then_inc(S["pre_act"], 1)
                        else:
                            A(m["qw"][:, :], st[:, 0, :], ACT.Sigmoid)
                            A(m["kw"][:, :], st[:, 1, :], ACT.Sigmoid)
                            A(m["vw"][:, 0, 0:T], st[:, 2, :], ACT.Copy)
                            act.drain().then_inc(S["pre_act"], 1)

                    def logs(with_logs=None, with_exp=None):
                        if not gla:
                            hold("act", S["forget_made"], j + 1)
                            A(m["bw"][:, :], m["bw"][:, :], ACT.Ln)
                            A(m["e1"][:, :], m["e1"][:, :], ACT.Ln)
                            act.drain().then_inc(S["logs_made"], 1)
                            if with_logs:
                                with_logs()
                        hold("act", S["b_ready"], g + 1)
                        act.drain()
                        A(m["e1"][:, :], m["bw"][:, :], ACT.Exp, scale=scale).then_inc(S["e1_ready"], 1)
                        if with_exp:
                            with_exp()

                    def exps():
                        hold("act", S["kd_diff"], g + 1)
                        A(m["kd"][:, 0:T], m["kd"][:, 0:T], ACT.Exp, scale=scale).then_inc(S["kd_exp"], 1)
                        for n in range(LV - 1):
                            hold("act", S["tree_diff"], (LV - 1) * g + (n + 1))
                            t = TP if n < 2 else T
                            A(m["xl"][:, n, 0:t], m["xl"][:, n, 0:t], ACT.Exp, scale=scale).then_inc(S["tree_exp"], 1)
                        if not gla:
                            hold("act", S["st_ready"], 4 * g + 4)
                            A(m["gn"][:, :], st[:, 3, :], ACT.Sigmoid).then_inc(S["gn_ready"], 1)

                    def turned():
                        for v in range(nv + 1):
                            hold("act", S["turned"], (nv + 1) * j + (t0 + v + 1))
                            dst = m["vt"][:, :, v * P:(v + 1) * P] if v < nv else m["kt"][:, :, :]
                            b = 2 * (v % 2)
                            A(dst[:, 0:NC, :], PM[:, b, :].rearrange("p (c k) -> p c k", c=NC), ACT.Copy)
                            A(dst[:, NC, :], PM[:, b + 1, 0:P], ACT.Copy)
                            act.drain().then_inc(S["turned_read"], 1)

                    def copy_out():
                        hold("act", S["o_psum"], g + 1)
                        hold("act", S["head_out"], g + 1)
                        for v in range(nv):
                            for dst, f in ((m["o"], ACT.Copy), (m["sq"], ACT.Square)):
                                A(dst[:, v, 0:TP], PM[:, v, :], f)
                                A(dst[:, v, TP:T], PM[:, 2, v * TS:(v + 1) * TS], f)
                        act.drain().then_inc(S["o_copied"], 1)
                        pre_ = "gla" if gla else "hgrn"
                        act.dma_start(o[pre_ + "_p"][0, 0][ds(j, 1), :, :].rearrange("h k v -> k (h v)"), m["s"][:, NC - 1, :]).then_inc(S["sp_stored"], 16)
                        act.dma_start(o[pre_ + "_s"][0, 0][ds(j, 1), :, :].rearrange("h k v -> k (h v)"), m["s"][:, NC, :]).then_inc(S["ss_stored"], 16)

                    def rstd_log():
                        hold("act", S["o_mean"], g + 1)
                        A(two(m["rh"][:, :]), PM[:, 2:4, 0:HT], ACT.Ln, scale=1.0 / (nv * P), bias=eps[:, 0:1])
                        act.drain()

                    def rstd_exp():
                        A(m["rh"][:, :], m["rh"][:, :], ACT.Exp, scale=-0.5).then_inc(S["o_rstd"], 1)

                    def out_hi():
                        hold("act", S["o_scaled"], j + 1)
                        A(tile(COH, j), m["o"][:, 0, :], ACT.Copy).then_inc(S["oh_ready"], 1)

                    def levels_done():
                        hold("act", S["level_placed"], LV * g + LV)
                    return load_state, pre, logs, exps, turned, levels_done, copy_out, rstd_log, rstd_exp, out_hi

                def gla_head(h, last=False):
                    load_state, pre, logs, exps, turned, _, copy_out, rstd_log, rstd_exp, _ = scan(h - 1)
                    for b, parts in enumerate(((load_state, pre, logs), (exps,), (), (turned, copy_out), (rstd_log, rstd_exp))):
                        for part in parts:
                            part()
                        if b < 4 and not last:
                            hi(u0 + b + 2, h, KT)

                def hgrn_head(h, last=False):
                    _, _, _, exps, turned, levels_done, copy_out, rstd_log, rstd_exp, out_hi = scan(h - 1)
                    if last:
                        for part in (exps, turned, copy_out, rstd_log, rstd_exp, out_hi):
                            part()
                        return
                    hi(u0 + 2, h, KT)
                    exps()
                    hi(u0 + 3, h, KT)
                    hi(u0 + 4, h, KT)
                    turned()
                    levels_done()
                    load_state, pre, logs = scan(h)[0:3]
                    pre()
                    copy_out()
                    load_state()
                    logs(lambda: (hi(u0 + 5, h, KT), rstd_log()), rstd_exp)
                    out_hi()

                for b in range(4):
                    hi(u0 + b + 2, 0, KT)
                head = gla_head if gla else hgrn_head
                if not gla:
                    for part in scan(0)[0:3]:
                        part()
                loop("act", 1, nh, head)
                head(nh, last=True)

            act.sem_inc(S["sp_stored"], 16)
            act.sem_inc(S["ss_stored"], 16)
            heads("ab_heads", 4, GM, 0, 1.0 / 16.0, 0)

            def gate(i, b):
                hold("act", S["g_scaled"], 4 * i + (b + 1))
                A(GS[:, :], GG[:, :], ACT.Silu).then_inc(S["gs_ready"], 1)
                hold("act", S["go_made"], 4 * i + (b + 1))
                A(tile(GOH, 4 * i + b), GG[:, :], ACT.Copy).then_inc(S["goh_ready"], 1)
            run("ab_g", gate)
            run("ab_outo", lambda i, b: x_out(2, 4 * i + b))
            rms(2)
            ffn("l0f2", 3)
            ffn("l1f1", 4)
            heads("c_heads", 8, CM, 4, 1.0, 12)
            run("c_out", lambda i, b: x_out(5, 4 * i + b))
            rms(5)
            ffn("l1f2", 6, final=True)
            for c in range(NC + 1):
                act.wait_ge(S["yt_psum"], c + 1)
                if c >= 2:
                    act.wait_ge(y_stored[c % 2], 16 * (c // 2))
                A(yout[:, c % 2, :], PM[:, 2 * (c % 2):2 * (c % 2) + 2, :].rearrange("p s t -> p (s t)"), ACT.Copy).then_inc(S["yt_copied"], 1)

        @block.vector
        def _(dve):
            TT, STT, TSC = dve.tensor_tensor, dve.scalar_tensor_tensor, dve.tensor_scalar

            def run(name, evac):
                u0, n, _ = plan[name]

                def body(i):
                    for b in range(min(2, n)):
                        hold("dve", S["unit_done"], 2 * i + (u0 + b + 1 + CREDIT))
                        evac(2 * i + b, u0 + b, b)
                loop("dve", 0, max(n // 2, 1), body)

            def x_out(e, m, final=False):
                if not final:
                    hold("dve", S["xh_ready"], m + (e * KT + 1))
                    STT(tile(XL, m), tile(H, m), vec[:, ds(m + NORM_COL[e], 1)], tile(XH, m).bitcast(F),
                        ALU.mult, ALU.subtract).then_inc(S["xl_ready"], 1)
                hold("dve", S["sq_ready"], m + (e * KT + 1))
                TT(ACC[:, :], ACC[:, :], SQ[:, :], ALU.add)
                dve.drain().then_inc(S["acc_done"], 1)

            def clear_acc():
                dve.memset(ACC[:, :], 0.0)
                dve.drain().then_inc(S["acc_done"], 1)

            def residual(e, scale, with_x, final=False):
                def evac(m, ps, b):
                    STT(two(tile(H, m)), pair(ps), scale, two(tile(H, m)), ALU.mult, ALU.add)
                    dve.drain().then_inc(S["pair_read"], 1)
                    if with_x:
                        dve.sem_inc(S["h_ready"], 1)
                        x_out(e, m, final)
                return evac

            hidden = [0]

            def ffn(tag, e, final=False):
                dve.wait_ge(S["rs_ready"], e)
                for g, (f0, nf) in enumerate(GROUPS):
                    base = hidden[0]

                    def up(u, ps, b):
                        if b == 0:
                            TT(two(TG[:, :]), pair(ps), two(RS[:, :]), ALU.mult).then_inc(S["gate_scaled"], 1)
                            dve.drain().then_inc(S["pair_read"], 1)
                            return
                        TT(two(TU[:, :]), pair(ps), two(RS[:, :]), ALU.mult)
                        dve.drain().then_inc(S["pair_read"], 1)
                    u0, n, _ = plan[f"{tag}_up{g}"]

                    def body(i):
                        for b in range(2):
                            hold("dve", S["unit_done"], 2 * i + (u0 + b + 1 + CREDIT))
                            up(None, u0 + b, b)
                        hold("dve", S["silu_done"], i + (base + 1))
                        TT(AV[:, :], TG[:, :], TU[:, :], ALU.mult).then_inc(S["act_made"], 1)
                        dve.drain()
                        hold("dve", S["ah_ready"], i + (base + 1))
                        TT(tile(AL, i), AV[:, :], tile(AH, i).bitcast(F), ALU.subtract).then_inc(S["al_ready"], 1)
                        dve.drain()
                    loop("dve", 0, nf, body)
                    hidden[0] += nf
                    if g:
                        clear_acc()
                    run(f"{tag}_down{g}", residual(e, 0.5, g == 1, final))

            dve.sem_inc(S["pair_read"], CREDIT)
            dve.wait_ge(S["vec_ready"], 1)
            TT(LB[:, 0, :], vec[:, V_LB:V_LB + KT], vec[:, V_LB:V_LB + KT], ALU.subtract).then_inc(S["lb_in"], 1)
            dve.wait_ge(S["lb_exp"], 1)
            dve.reciprocal(LB[:, 2, :], LB[:, 1, :])
            dve.drain()
            TT(LB[:, 1, :], LB[:, 1, :], LB[:, 2, :], ALU.mult)
            dve.drain()
            TT(LB[:, 2, :], LB[:, 1, :], LB[:, 1, :], ALU.subtract)
            dve.drain()
            TSC(LB[:, 3, :], LB[:, 2, :], -1.0, 1.0, ALU.mult, ALU.add)
            clear_acc()
            for m in range(KT):
                dve.wait_ge(S["x_psum"], m + 1)
                b = 2 * (m % 2)
                dve.tensor_copy(H[:, m, 0:TP], PM[:, b, :])
                dve.tensor_copy(H[:, m, TP:T], PM[:, b + 1, 0:TS])
                dve.drain().then_inc(S["h_ready"], 1)
                x_out(0, m)
            ffn("l0f1", 1)

            dve.wait_ge(S["rs_ready"], 2)

            def small(m, ps, b):
                TT(two(DTG[0:64, :]), pair(ps)[0:64], two(RS[0:64, :]), ALU.mult)
                dve.drain().then_inc(S["pair_read"], 1)
            run("ab_small", small)
            dve.wait_ge(S["ab_masks"], 1)

            def xbc(m, ps, b):
                e, cv, s0, s1 = XE[b], CV[b], PD[:, 2 * (ps % 2), :], PD[:, 2 * (ps % 2) + 1, :]
                TT(e[:, 3:3 + HT], s0[:, 0:HT], RS[:, 0:HT], ALU.mult)
                TT(e[:, 3 + HT:3 + TP], s1[:, 0:TP - HT], RS[:, HT:TP], ALU.mult)
                TT(e[:, TP + 6:T + 6], s1[:, TP - HT:HT], RS[:, TP:T], ALU.mult)
                dve.tensor_copy(e[:, TP + 3:TP + 6], cst[:, :].rearrange("p (r c) -> p c r", r=3)[:, ds(m, 1), :].rearrange("p a r -> p (a r)"))
                dve.drain().then_inc(S["pair_read"], 1)
                hold("dve", S["xc_ready"], m + 1)
                TSC(cv[:, :], e[:, 0:T + 3], vec[:, ds(m + V_CW, 1)], vec[:, ds(m + V_CB, 1)], ALU.mult, ALU.add)
                for k in range(1, 4):
                    dve.drain()
                    last = STT(cv[:, :], e[:, k:k + T + 3], vec[:, ds(m + (V_CW + NXT * k), 1)], cv[:, :], ALU.mult, ALU.add)
                last.then_inc(S["conv_ready"], 1)
                keep = XLAST[:, 0:6 * NXT].rearrange("p (r c) -> p c r", r=6)[:, ds(m, 1), :].rearrange("p a r -> p (a r)")
                dve.tensor_copy(keep[:, 0:3], e[:, TP:TP + 3])
                dve.tensor_copy(keep[:, 3:6], e[:, T + 3:T + 6])
                dve.drain()
            run("ab_xbc", xbc)
            dve.sem_inc(S["last_rows"], 1)

            def z(m, ps, b):
                TT(two(tile(SZ, m)), pair(ps), two(RS[:, :]), ALU.mult).then_inc(S["z_scaled"], 1)
                dve.drain().then_inc(S["pair_read"], 1)
            run("ab_z", z)

            d = [DTW[0:HA, n, :] for n in range(7)]
            dve.wait_ge(S["small_landed"], 48)
            TSC(d[0], DTG[0:HA, :], DTW[0:HA, 7, 0:1], None, ALU.add)
            dve.drain()
            STT(d[1], d[0], -1.0, d[0], ALU.mult, ALU.max).then_inc(S["dt_abs"], 1)
            dve.wait_ge(S["dt_exp"], 1)
            TSC(d[3], d[2], 1.0, None, ALU.add).then_inc(S["dt_plus"], 1)
            dve.drain()
            TSC(d[5], d[3], -1.0, None, ALU.add)
            dve.drain()
            TSC(d[6], d[5], 0.0, None, ALU.is_equal)
            dve.drain()
            TT(d[5], d[5], d[6], ALU.add)
            dve.drain()
            dve.reciprocal(d[5], d[5])
            dve.wait_ge(S["dt_log"], 1)
            TT(d[4], d[4], d[6], ALU.add)
            dve.drain()
            TT(d[4], d[4], d[2], ALU.mult)
            dve.drain()
            TT(d[4], d[4], d[5], ALU.mult)
            dve.drain()
            STT(d[4], d[0], 0.0, d[4], ALU.max, ALU.add)
            dve.drain()
            TSC(d[5], d[4], DTW[0:HA, 7, 2:3], -1.0, ALU.mult, ALU.mult)
            dve.memset(d[6], 1.0)
            dve.drain()
            dve.memset(d[6][:, 0:T:CH], 0.0)
            dve.drain()
            dve.tensor_tensor_scan(d[3], d[6], d[5], 0.0, ALU.mult, ALU.add)
            dve.memset(DC[:, :], 0.0)
            dve.drain()
            dve.tensor_copy(DC[0:HA, :], d[4])
            dve.tensor_copy(DC[32:32 + HA, :], d[3])
            dve.drain().then_inc(S["ssd_ready"], 1)
            dve.wait_ge(S["sz_ready"], KT)
            dve.sem_inc(S["ssd_ready"], 1)
            dve.wait_ge(S["ssd_ready"], 3)
            dve.sem_inc(S["yl_ready"], 1)
            dve.sem_inc(S["state_new"], 1)

            def heads_over(x, n):
                return x.unsqueeze(2).broadcast_to([P, x.shape[1], n])

            def chunk(c, t0):
                n = CH if not isinstance(c, int) else TS
                hold("dve", S["chunk_turned"], c + 1)
                dve.tensor_copy(DCT[:, :], PM[:, 2, 2 * P:3 * P])
                dve.tensor_copy(BT[:, :], PM[:, 2, 0:2 * P])
                TSC(CE[32:48, :], ident[32:48, 32:48], DCC[32:48, n - 1:n], None, ALU.mult)
                dve.drain().then_inc(S["chunk_dct"], 1)
                hold("dve", S["end_psum"], c + 1)
                dve.tensor_copy(EE[:, :], PM[:, 2, 384:384 + HA])
                TT(DE[:, :], PM[:, 2, 384:384 + HA], DCT[:, 32:48], ALU.subtract)
                dve.drain()
                TSC(DE[:, :], DE[:, :], 0.0, None, ALU.min)
                dve.drain().then_inc(S["end_diff"], 1)
                xd = XD[:, :].rearrange("p (h q) -> p h q", q=PA)
                TT(xd, PM[:, 0:2, :].rearrange("p s (h q) -> p (s h) q", q=PA), heads_over(DCT[:, 0:HA], PA), ALU.mult)
                dve.drain()
                hold("dve", S["end_exp"], c + 1)
                TT(XDE[:, :].rearrange("p (h q) -> p h q", q=PA), xd, heads_over(DE[:, :], PA), ALU.mult)
                dve.drain().then_inc(S["x_scaled"], 1)
                hold("dve", S["cb_psum"], c + 1)
                TT(CBM[:, :, :], PM[:, 3, 0:2 * CH].rearrange("p (g t) -> p g t", g=2),
                   TRI[:, :].unsqueeze(1).broadcast_to([P, 2, CH]), ALU.mult).then_inc(S["cb_masked"], 1)
                for q in range(4):
                    hold("dve", S["cum_psum"], 4 * c + (q + 1))
                    TT(LM[:, q], PD[:, q, :].rearrange("p (h t) -> p h t", h=4), heads_over(DCT[:, 32 + 4 * q:36 + 4 * q], CH), ALU.subtract)
                    dve.drain()
                    TSC(LM[:, q], LM[:, q], 0.0, None, ALU.min).then_inc(S["cum_diff"], 1)
                for q in range(4):
                    hold("dve", S["decay_exp"], 4 * c + (q + 1))
                    TT(LM[:, q], LM[:, q], CBM[:, q // 2, :].unsqueeze(1).broadcast_to([P, 4, CH]), ALU.mult).then_inc(S["decay_made"], 1)
                hold("dve", S["y_psum"], c + 1)
                hold("dve", S["spread_exp"], c + 1)
                TT(Y[:, :, :], PD[:, 2:4, :].rearrange("p s (m t) -> p (s m) t", t=CH), EP[:, :, :], ALU.mult)
                dve.drain()
                TT(Y[:, :, :], PD[:, 0:2, :].rearrange("p s (m t) -> p (s m) t", t=CH), Y[:, :, :], ALU.add)
                dve.drain()
                for m in range(KT):
                    STT(Y[:, m, :], XCC[:, m, :], DCOL[:, m:m + 1], Y[:, m, :], ALU.mult, ALU.add)
                dve.drain()
                TT(Y[:, :, 0:n], Y[:, :, 0:n], SZ[:, :, ds(t0, n)], ALU.mult)
                dve.drain().then_inc(S["y_gated"], 1)
                hold("dve", S["state_psum"], c + 1)
                hs = HS[:, :].rearrange("p (h q) -> p h q", q=PA)
                TT(hs, hs, heads_over(EE[:, :], PA), ALU.mult)
                dve.drain()
                TT(HS[:, :], PM[:, 0:2, :].rearrange("p s t -> p (s t)"), HS[:, :], ALU.add)
                dve.drain().then_inc(S["state_new"], 1)
                hold("dve", S["y_rstd"], c + 1)
                for g in range(2):
                    TT(Y[:, 4 * g:4 * g + 4, :], Y[:, 4 * g:4 * g + 4, :], RY[:, g, :].unsqueeze(1).broadcast_to([P, 4, CH]), ALU.mult)
                dve.drain()
                TT(Y[:, :, :], Y[:, :, :], heads_over(vec[:, V_SN:V_SN + KT], CH), ALU.mult)
                dve.drain().then_inc(S["y_weighted"], 1)
                hold("dve", S["yh_ready"], c + 1)
                TT(YL[:, :, ds(t0, n)], Y[:, :, 0:n], YH[:, :, ds(t0, n)].bitcast(F), ALU.subtract).then_inc(S["yl_ready"], 1)

            with dve.Fori(0, NC) as c:
                chunk(c, c * CH)
            dve.wait_ge(S["h0_ready"], 2)
            chunk(NC, TP)
            run("ab_outy", residual(1, 1.0, False))

            def heads(name, nh, m, g0, weights, first):
                u0 = plan[name][0]
                nv = m["nv"]
                gla = nv == 2
                b_, q_, k_ = m["bw"], m["qw"], m["kw"]

                def units(h, b):
                    hold("dve", S["unit_done"], 4 * h + (u0 + b + 1 + CREDIT))
                    TT(two(m["st"][:, b, :]), pair(u0 + b), two(RS[:, :]), ALU.mult).then_inc(S["st_ready"], 1)
                    dve.drain().then_inc(S["pair_read"], 1)

                def scan(j):
                    g = j + g0

                    def pre():
                        hold("dve", S["pre_act"], g + 1)
                        if gla:
                            STT(m["gw"][:, :], m["gw"][:, :], 0.0, m["e1"][:, :], ALU.min, ALU.subtract)
                        else:
                            TT(q_[:, :], q_[:, :], m["st"][:, 0, :], ALU.mult)
                            TSC(m["gw"][:, :], k_[:, :], LB[:, 3, ds(j, 1)], LB[:, 2, ds(j, 1)], ALU.mult, ALU.add)
                            dve.drain()
                            TSC(b_[:, :], m["gw"][:, :], 2.0 ** -60, None, ALU.max)
                            TSC(m["e1"][:, :], m["gw"][:, :], TINY, 2.0 ** 60, ALU.max, ALU.mult)
                            dve.drain()
                            TSC(m["e1"][:, :], m["e1"][:, :], 1.0, None, ALU.min)
                            TSC(k_[:, :], m["gw"][:, :], -1.0, 1.0, ALU.mult, ALU.add)
                            dve.drain().then_inc(S["forget_made"], 1)
                            hold("dve", S["logs_made"], j + 1)
                            TT(m["gw"][:, :], b_[:, :], m["e1"][:, :], ALU.add)
                        dve.drain()
                        dve.tensor_tensor_scan(b_[:, :], m["rm"][:, :], m["gw"][:, :], 0.0, ALU.mult, ALU.add).then_inc(S["b_ready"], 1)
                        dve.drain()

                    def diffs():
                        bc = b_[:, 0:TP].rearrange("p (c t) -> p c t", c=NC)
                        TT(m["kd"][:, 0:TP].rearrange("p (c t) -> p c t", c=NC), bc[:, :, CH - 1:CH].broadcast_to([P, NC, CH]), bc, ALU.subtract)
                        TT(m["kd"][:, TP:T], b_[:, T - 1:T].broadcast_to([P, TS]), b_[:, TP:T], ALU.subtract)
                        dve.drain().then_inc(S["kd_diff"], 1)
                        for n, hf in enumerate(TREE):
                            t = TP if n < 2 else T
                            bn = b_[:, 0:t].rearrange("p (n s r) -> p n s r", s=2, r=hf)
                            xn = m["xl"][:, n, 0:t].rearrange("p (n s r) -> p n s r", s=2, r=hf)
                            mid = bn[:, :, 0, hf - 1:hf].broadcast_to([P, t // (2 * hf), hf])
                            TT(xn[:, :, 0, :], mid, bn[:, :, 0, :], ALU.subtract)
                            TT(xn[:, :, 1, :], bn[:, :, 1, :], mid, ALU.subtract)
                            dve.drain().then_inc(S["tree_diff"], 1)
                        hold("dve", S["e1_ready"], g + 1)
                        TT(m["qe"][:, :], m["e1"][:, :], q_[:, :], ALU.mult)
                        dve.tensor_copy(m["et"][:, 0:NC], m["e1"][:, CH - 1:TP:CH])
                        dve.tensor_copy(m["et"][:, NC:NC + 1], m["e1"][:, T - 1:T])
                        hold("dve", S["kd_exp"], g + 1)
                        TT(m["kd"][:, 0:T], m["kd"][:, 0:T], k_[:, :], ALU.mult)
                        dve.drain().then_inc(S["kd_ready"], 1)

                    def products():
                        for n, hf in enumerate(TREE):
                            t = TP if n < 2 else T
                            hold("dve", S["tree_exp"], (LV - 1) * g + (n + 1))
                            xn = m["xl"][:, n, 0:t].rearrange("p (n s r) -> p n s r", s=2, r=hf)
                            for s, y in ((0, k_), (1, q_)):
                                yn = y[:, 0:t].rearrange("p (n s r) -> p n s r", s=2, r=hf)
                                TT(xn[:, :, s, :], xn[:, :, s, :], yn[:, :, s, :], ALU.mult)
                            dve.drain().then_inc(S["tree_made"], 1)
                        if not gla:
                            hold("dve", S["gn_ready"], j + 1)
                            TT(m["gs"][:, :], m["gn"][:, :], m["st"][:, 3, :], ALU.mult)
                            dve.drain()

                    def levels():
                        for n in range(LV):
                            hold("dve", S["level_psum"], LV * g + (n + 1))
                            src = PM[:, n % 2, :].rearrange("p (c t) -> p c t", c=NC)
                            if n == 0:
                                dve.tensor_copy(m["att"][0:64, :, 64:128], src[0:64, :, 64:128])
                            elif n == 1:
                                for e in range(2):
                                    dve.tensor_copy(m["att"][64 * e:64 * e + 32, :, 64 * e + 32:64 * e + 64],
                                                    src[64 * e:64 * e + 32, :, 64 * e + 32:64 * e + 64])
                            else:
                                mk = m["mask"][:, n - 2, :] if n < LV - 1 else ident[:, :]
                                dve.copy_predicated(m["att"][:, :, :], mk.bitcast(I32).unsqueeze(1).broadcast_to([P, NC, CH]), src)
                                dve.copy_predicated(m["ats"][0:TS, :], mk[0:TS, 0:TS].bitcast(I32), PM[0:TS, 2 + n % 2, 0:TS])
                            dve.drain().then_inc(S["level_placed"], 1)

                    def states():
                        hold("dve", S["kv_psum"], g + 1)
                        hold("dve", S["s0_landed"], 16 * g + 16)
                        hold("dve", S["sp_stored"], 16 * g + 16)
                        hold("dve", S["ss_stored"], 16 * g + 16)
                        per = 4 // nv

                        def kv(c):
                            return PM[:, c // per, (c % per) * nv * P:(c % per + 1) * nv * P]
                        dve.tensor_copy(m["s"][:, 0, :], kv(0))
                        STT(m["s"][:, NC, :], m["si"][:, :], m["et"][:, NC:NC + 1], kv(NC), ALU.mult, ALU.add)
                        for c in range(1, NC):
                            dve.drain()
                            STT(m["s"][:, c, :], m["s"][:, c - 1, :], m["et"][:, c:c + 1], kv(c), ALU.mult, ALU.add)
                        dve.drain().then_inc(S["s_ready"], 1)

                    def out():
                        hold("dve", S["o_rstd"], g + 1)
                        for v in range(nv):
                            dst = tile(ON, 2 * j + v) if gla else m["o"][:, v, :]
                            STT(dst, m["o"][:, v, :], vec[:, weights + v:weights + v + 1], m["rh"][:, :], ALU.mult, ALU.mult)
                        if gla:
                            dve.drain().then_inc(S["head_out"], 1)
                            return
                        dve.drain()
                        TT(m["o"][:, 0, :], m["o"][:, 0, :], m["gs"][:, :], ALU.mult).then_inc(S["o_scaled"], 1)
                        dve.drain()
                        hold("dve", S["oh_ready"], j + 1)
                        TT(tile(COL, j), m["o"][:, 0, :], tile(COH, j).bitcast(F), ALU.subtract)
                        dve.drain().then_inc(S["head_out"], 1)

                    def place_levels():
                        levels()
                        states()
                    return pre, diffs, products, place_levels, out

                dve.wait_ge(S["scan_consts_made"], first)
                for b in range(4):
                    units(0, b)

                def gla_body(h):
                    parts = scan(h - 1)
                    for b in range(4):
                        parts[b]()
                        units(h, b)
                    parts[4]()

                def hgrn_body(h):
                    _, diffs, products, place_levels, out = scan(h - 1)
                    diffs()
                    units(h, 0)
                    products()
                    units(h, 1)
                    units(h, 2)
                    place_levels()
                    scan(h)[0]()
                    units(h, 3)
                    out()
                if not gla:
                    scan(0)[0]()
                loop("dve", 1, nh, gla_body if gla else hgrn_body)
                for part in scan(nh - 1)[0 if gla else 1:]:
                    part()
                dve.wait_ge(S["sp_stored"], 16 * (g0 + nh + 1))
                dve.wait_ge(S["ss_stored"], 16 * (g0 + nh + 1))

            dve.wait_ge(S["rs_ready"], 2)
            dve.sem_inc(S["head_out"], 1)
            heads("ab_heads", 4, GM, 0, V_GN, 1)

            def gate(m, ps, b):
                TT(two(GG[:, :]), pair(ps), two(RS[:, :]), ALU.mult).then_inc(S["g_scaled"], 1)
                dve.drain().then_inc(S["pair_read"], 1)
                hold("dve", S["gs_ready"], m + 1)
                TT(GG[:, :], GS[:, :], tile(ON, m), ALU.mult).then_inc(S["go_made"], 1)
                dve.drain()
                hold("dve", S["goh_ready"], m + 1)
                TT(tile(GOL, m), GG[:, :], tile(GOH, m).bitcast(F), ALU.subtract)
                dve.drain().then_inc(S["gol_ready"], 1)
            run("ab_g", gate)
            clear_acc()
            run("ab_outo", residual(2, 1.0, True))
            ffn("l0f2", 3)
            ffn("l1f1", 4)
            dve.wait_ge(S["rs_ready"], 5)
            heads("c_heads", 8, CM, 4, V_HN, 2)
            clear_acc()
            run("c_out", residual(5, 1.0, True))
            ffn("l1f2", 6, final=True)
            dve.wait_ge(S["rs_ready"], 7)
            dve.memset(YF[:, :, T:TPAD], 0.0)
            for m in range(KT):
                STT(YF[:, m, 0:T], H[:, m, :], vec[:, V_FIN + m:V_FIN + m + 1], RS[:, :], ALU.mult, ALU.mult)
            dve.drain().then_inc(S["y_ready"], 1)

        @block.tensor
        def _(pe):
            mm = pe.matmul

            def unit(ps, i, k, rh, rl, before=None):
                hold("pe", S["lo_ready"], 2 * i + (ps + 1 + CREDIT))
                hold("pe", S["pair_read"], 2 * i + (ps - 1 + CREDIT))
                for p, (wt, x) in enumerate(((whi, rh), (whi, rl), (wlo, rh))):
                    for r in range(k):
                        if before:
                            before(p, r)
                        for s in range(2):
                            last = mm(PD[:, 2 * (ps % 2) + s, 0:HT], wt[ps % 2][:, r, :], x[:, r, s * HT:(s + 1) * HT],
                                      start=(p == 0 and r == 0), stop=(p == 2 and r == k - 1))
                last.then_inc(S["unit_done"], 1)

            def run(name, rh, rl, before=None, after_first=None):
                u0, n, k = plan[name]
                unit(u0, 0, k, rh, rl, before)
                if after_first:
                    after_first()
                if n > 1:
                    unit(u0 + 1, 0, k, rh, rl)
                    loop("pe", 1, n // 2, lambda i: (unit(u0, i, k, rh, rl), unit(u0 + 1, i, k, rh, rl)))

            def parts_of(hs, ls, hbase, lbase):
                def before(p, r):
                    if p < 2:
                        pe.wait_ge((hs, ls)[p], (hbase, lbase)[p] + r + 1)
                return before

            def mean_square(e):
                pe.wait_ge(S["acc_done"], 9 * e + 9)
                for s in range(2):
                    last = mm(PM[:, s, 0:HT], ones[:, :], ACC[:, s * HT:(s + 1) * HT], start=True, stop=True)
                last.then_inc(S["ms_ready"], 1)

            def x_parts(e):
                return parts_of(S["xh_ready"], S["xl_ready"], e * KT, e * KT)

            hidden = [0]

            def ffn(tag, e):
                for g, (_, nf) in enumerate(GROUPS):
                    if g == 0:
                        run(f"{tag}_up{g}", XH, XL, x_parts(e), lambda: mean_square(e))
                    else:
                        run(f"{tag}_up{g}", XH, XL)
                    run(f"{tag}_down{g}", AH, AL, parts_of(S["ah_ready"], S["al_ready"], hidden[0], hidden[0]))
                    hidden[0] += nf

            pe.sem_inc(S["unit_done"], CREDIT)
            pe.wait_ge(S["consts_made"], 2)
            pe.wait_ge(S["rows_landed"], 16 * 12)
            for n in range(3):
                last = pe.transpose(PM[:, 2, n * P:(n + 1) * P], rows[:, n, :], ident[:, :])
            last.then_inc(S["vec_psum"], 1)
            pe.wait_ge(S["vec_ready"], 1)
            pe.wait_ge(x_landed[0], 16)
            pe.wait_ge(x_landed[1], 16)
            for m in range(KT):
                if m >= 2:
                    pe.wait_ge(S["h_ready"], m - 1)
                b = 2 * (m % 2)
                for c in range(NC):
                    pe.transpose(PM[:, b, c * P:(c + 1) * P], xin[:, c, m * P:(m + 1) * P], ident[:, :])
                mm(PM[:, b + 1, 0:TS], xin[0:TS, NC, m * P:(m + 1) * P], ident[0:TS, 0:TS], start=True, stop=True).then_inc(S["x_psum"], 1)
            ffn("l0f1", 0)

            run("ab_small", XH, XL, x_parts(1), lambda: mean_square(1))
            run("ab_xbc", XH, XL)
            run("ab_z", XH, XL)
            pe.wait_ge(S["rs_ready"], 2)
            pe.wait_ge(S["last_rows"], 1)
            pe.transpose(PM[:, 2, 0:P], XLAST[:, :], ident[:, :]).then_inc(S["last_psum"], 1)

            def turn_state(k, banks):
                for m in range(KT):
                    src = HS[:, m * P:(m + 1) * P] if banks == 0 else HIO[:, m, :]
                    last = pe.transpose(PM[:, banks + m // 4, (m % 4) * P:(m % 4 + 1) * P], src, ident[:, :])
                last.then_inc(S["hout_psum"] if banks == 0 else S["h0_psum"], 1)

            def chunk(c, n):
                hold("pe", S["chunk_copied"], c + 1)
                for m in range(KT):
                    pe.transpose(PM[:, m // 4, (m % 4) * P:(m % 4 + 1) * P], XCC[:, m, :], ident[:, :])
                for g in range(2):
                    pe.transpose(PM[:, 2, g * P:(g + 1) * P], XCC[:, KT + g, :], ident[:, :])
                pe.transpose(PM[:, 2, 2 * P:3 * P], DCC[:, :], ident[:, :]).then_inc(S["chunk_turned"], 1)
                for g in range(2):
                    last = mm(PM[:, 3, g * CH:(g + 1) * CH], XCC[:, KT + g, :], XCC[:, KT + 2 + g, :], start=True, stop=True)
                last.then_inc(S["cb_psum"], 1)
                for h in range(HA):
                    last = mm(PD[:, h // 4, (h % 4) * CH:(h % 4 + 1) * CH], SEL[0:64, h, :], DCC[0:64, :], start=True, stop=True)
                    if h % 4 == 3:
                        last.then_inc(S["cum_psum"], 1)
                hold("pe", S["chunk_dct"], c + 1)
                mm(PM[:, 2, 384:384 + HA], ones[32:48, :], CE[32:48, :], start=True, stop=True).then_inc(S["end_psum"], 1)
                hold("pe", S["x_scaled"], c + 1)
                for m in range(KT):
                    last = mm(PM[:, m // 4, (m % 4) * CH:(m % 4 + 1) * CH], SELP[0:64, m, :], DCC[0:64, :], start=True, stop=True)
                last.then_inc(S["spread_psum"], 1)
                hold("pe", S["decay_exp"], 4 * c + 4)
                for m in range(KT):
                    mm(PD[:, 2 + m // 4, (m % 4) * CH:(m % 4 + 1) * CH], HS[:, m * P:(m + 1) * P], XCC[:, KT + 2 + m // 4, :], start=True, stop=True)
                for h in range(HA):
                    if h % 4 == 0:
                        hold("pe", S["decay_made"], 4 * c + (h // 4 + 1))
                    m, e = h // 2, h % 2
                    last = mm(PD[e * PA:(e + 1) * PA, m // 4, (m % 4) * CH:(m % 4 + 1) * CH], XD[:, h * PA:(h + 1) * PA],
                              LM[:, h // 4, h % 4, :], start=True, stop=True)
                last.then_inc(S["y_psum"], 1)
                hold("pe", S["spread_exp"], c + 1)
                for g in range(2):
                    last = mm(PM[:, g, :], BT[0:n, g * P:(g + 1) * P], XDE[0:n, g * 512:(g + 1) * 512], start=True, stop=True)
                last.then_inc(S["state_psum"], 1)
                hold("pe", S["y_squared"], c + 1)
                for g in range(2):
                    for m in range(4):
                        last = mm(PM[:, 2, g * CH:(g + 1) * CH], ones[:, :], EP[:, 4 * g + m, :], start=(m == 0), stop=(m == 3))
                last.then_inc(S["y_mean"], 1)

            pe.wait_ge(S["selectors"], 1)
            pe.wait_ge(S["d_landed"], 16)
            pe.wait_ge(S["last_copied"], 1)
            pe.wait_ge(S["pair_read"], plan["ab_outy"][0] + CREDIT)
            for m in range(KT):
                last = mm(PM[:, 3, m:m + 1], SELP[32:48, m, :], D16[32:48, 0:1], start=True, stop=True)
            last.then_inc(S["d_psum"], 1)
            pe.wait_ge(S["h0_ready"], 1)
            with pe.Fori(0, NC) as c:
                chunk(c, CH)
            pe.wait_ge(S["state_new"], NC + 1)
            turn_state(1, 0)
            pe.wait_ge(S["h0_landed"], 32)
            pe.wait_ge(S["y_rstd"], NC)
            turn_state(1, 2)
            pe.wait_ge(S["h0_ready"], 2)
            pe.wait_ge(S["hout_copied"], 1)
            chunk(NC, TS)
            pe.wait_ge(S["state_new"], NC + 2)
            turn_state(2, 0)
            pe.wait_ge(S["yh_ready"], NC + 1)
            pe.wait_ge(S["yl_ready"], NC + 2)
            run("ab_outy", YH, YL)

            def heads(name, nh, m, g0, t0, before=None, after_first=None):
                u0 = plan[name][0]
                nv = m["nv"]
                gla = nv == 2
                vt, kt, att, ats, s, si, qe = (m[x] for x in ("vt", "kt", "att", "ats", "s", "si", "qe"))

                def scan(j):
                    g = j + g0

                    def logits():
                        if gla:
                            hold("pe", S["wg_copied"], j + 1)
                            for e in range(2):
                                last = mm(PM[:, e, 0:HT], m["wg"][32:48, :], DTG[32:48, e * HT:(e + 1) * HT], start=True, stop=True)
                            last.then_inc(S["gk_psum"], 1)

                    def turn():
                        hold("pe", S["pre_act"], g + 1)
                        for v in range(nv + 1):
                            if v == nv:
                                hold("pe", S["kd_ready"], g + 1)
                            if v >= 2:
                                hold("pe", S["turned_read"], (nv + 1) * j + (t0 + v - 1))
                            src, b = (m["vw"][:, v, :] if v < nv else m["kd"][:, :]), 2 * (v % 2)
                            for c in range(NC):
                                pe.transpose(PM[:, b, c * P:(c + 1) * P], src[:, c * CH:(c + 1) * CH], ident[:, :])
                            pe.transpose(PM[:, b + 1, 0:P], src[:, TP:TPAD], ident[:, :]).then_inc(S["turned"], 1)

                    def tree():
                        hold("pe", S["turned_read"], (nv + 1) * j + (t0 + nv + 1))
                        for n in range(LV):
                            hf = TREE[n] if n < LV - 1 else 0
                            if n < LV - 1:
                                hold("pe", S["tree_made"], (LV - 1) * g + (n + 1))
                            if n >= 2:
                                hold("pe", S["level_placed"], LV * g + (n - 1))
                            if n < 2:
                                for k in range(TP // (2 * hf)):
                                    t = 2 * hf * k
                                    p = t % CH
                                    last = mm(PM[p:p + hf, n % 2, t + hf:t + 2 * hf], m["xl"][:, n, t:t + hf], m["xl"][:, n, t + hf:t + 2 * hf],
                                              start=True, stop=True)
                            else:
                                l, r = (m["xl"][:, n, :], m["xl"][:, n, :]) if hf else (m["kw"][:, :], m["qw"][:, :])
                                for c in range(NC):
                                    mm(PM[:, n % 2, c * CH:(c + 1) * CH], l[:, c * CH:(c + 1) * CH], r[:, c * CH:(c + 1) * CH], start=True, stop=True)
                                last = mm(PM[0:TS, 2 + n % 2, 0:TS], l[:, TP:T], r[:, TP:T], start=True, stop=True)
                            last.then_inc(S["level_psum"], 1)

                    def outputs():
                        hold("pe", S["level_placed"], LV * g + LV)
                        per = 4 // nv
                        for c in range(NC + 1):
                            last = mm(PM[:, c // per, (c % per) * nv * P:(c % per + 1) * nv * P], kt[:, c, :], vt[:, c, :], start=True, stop=True)
                        last.then_inc(S["kv_psum"], 1)
                        hold("pe", S["s_ready"], g + 1)
                        for v in range(nv):
                            vs = slice(v * P, (v + 1) * P)
                            for c in range(NC):
                                cs = slice(c * CH, (c + 1) * CH)
                                mm(PM[:, v, cs], vt[:, c, vs], att[:, c, :], start=True, stop=(c == 0))
                                if c:
                                    mm(PM[:, v, cs], s[:, c - 1, vs], qe[:, cs], start=False, stop=True)
                            mm(PM[:, 2, v * TS:(v + 1) * TS], vt[0:TS, NC, vs], ats[0:TS, :], start=True, stop=False)
                            last = mm(PM[:, 2, v * TS:(v + 1) * TS], si[:, vs], qe[:, TP:T], start=False, stop=True)
                        last.then_inc(S["o_psum"], 1)

                    def squares():
                        hold("pe", S["o_copied"], g + 1)
                        for e in range(2):
                            for v in range(nv):
                                last = mm(PM[:, 2 + e, 0:HT], ones[:, :], m["sq"][:, v, e * HT:(e + 1) * HT], start=(v == 0), stop=(v == nv - 1))
                        last.then_inc(S["o_mean"], 1)
                    return logits, turn, tree, outputs, squares

                for b in range(4):
                    unit(u0 + b, 0, KT, XH, XL, before if b == 0 else None)
                    if b == 0 and after_first:
                        after_first()

                def body(h):
                    logits, turn, tree, outputs, squares = scan(h - 1)
                    logits()
                    unit(u0, 2 * h, KT, XH, XL)
                    unit(u0 + 1, 2 * h, KT, XH, XL)
                    unit(u0 + 2, 2 * h, KT, XH, XL)
                    turn()
                    tree()
                    outputs()
                    unit(u0 + 3, 2 * h, KT, XH, XL)
                    squares()
                loop("pe", 1, nh, body)
                for part in scan(nh - 1):
                    part()

            heads("ab_heads", 4, GM, 0, 0)
            run("ab_g", XH, XL)
            run("ab_outo", GOH, GOL, parts_of(S["goh_ready"], S["gol_ready"], 0, 0))
            ffn("l0f2", 2)
            ffn("l1f1", 3)
            heads("c_heads", 8, CM, 4, 12, x_parts(4), lambda: (mean_square(4), pe.wait_ge(S["rs_ready"], 5)))
            pe.wait_ge(S["head_out"], 13)
            run("c_out", COH, COL)
            ffn("l1f2", 5)
            mean_square(6)
            pe.wait_ge(S["y_ready"], 1)
            for c in range(NC + 1):
                if c >= 2:
                    pe.wait_ge(S["yt_copied"], c - 1)
                b = 2 * (c % 2)
                for m in range(KT):
                    last = pe.transpose(PM[:, b + m // 4, (m % 4) * P:(m % 4 + 1) * P], YF[:, m, c * CH:(c + 1) * CH], ident[:, :])
                last.then_inc(S["yt_psum"], 1)


INPUTS = ["x_prompt", "x_sample", "state_ssm", "state_conv", "state_gla", "state_hgrn", "norm_ffn1", "ffn1_w_gu",
          "ffn1_w_down", "norm_mix", "ab_w_in", "ssm_conv_w", "ssm_conv_b", "ssm_dt_bias", "ssm_a_log", "ssm_d",
          "ssm_norm_w", "gla_w_gk", "gla_b_gk", "gla_norm_w", "ab_w_out", "c_w_in", "hgrn_lb_logits", "hgrn_norm_w",
          "c_w_out", "norm_ffn2", "ffn2_w_gu", "ffn2_w_down", "norm_final"]
OUTPUTS = [("y_p", (1, 512, 1024)), ("y_s", (1, 32, 1024)),
           ("ssm_p", (1, 1, 16, 64, 128)), ("conv_p", (1, 1, 3, 1536)), ("gla_p", (1, 1, 4, 128, 256)), ("hgrn_p", (1, 1, 8, 128, 128)),
           ("ssm_s", (1, 1, 16, 64, 128)), ("conv_s", (1, 1, 3, 1536)), ("gla_s", (1, 1, 4, 128, 256)), ("hgrn_s", (1, 1, 8, 128, 128))]


def kernel(**inputs):
    import numpy as np
    import concourse.bacc as bacc
    from concourse.bass_utils import run_bass_kernel_spmd

    nc = bacc.Bacc("TRN2", target_bir_lowering=False, num_devices=1)
    arrays, a, o = {}, {}, {}
    for name in INPUTS:
        x = np.ascontiguousarray(inputs[name])
        arrays["in_" + name] = x
        a[name] = nc.dram_tensor("in_" + name, x.shape, F, kind="ExternalInput").ap()
    for name, shape in OUTPUTS:
        o[name] = nc.dram_tensor("out_" + name, shape, F, kind="ExternalOutput").ap()
    build(nc, a, o)
    r = run_bass_kernel_spmd(nc, [arrays], core_ids=[0])
    return tuple(r.results[0]["out_" + name] for name, _ in OUTPUTS)
```

```python
from contextlib import ExitStack

import concourse.bass as bass
from concourse import mybir

F = mybir.dt.float32
FR = mybir.dt.float32r
I32 = mybir.dt.int32
ALU = mybir.AluOpType
ACT = mybir.ActivationFunctionType
ds = bass.ds

P = 128
D = 1024
KT = D // P
TP, TS = 512, 32
T = TP + TS
HT = T // 2
CH = 128
NC = TP // CH
TPAD = TP + CH
FF = 2816
FT = FF // P
GROUPS = [(0, 12), (12, 10)]
NXT = 12
HA, PA = 16, 64
COL_Z, COL_XBC, COL_DT, COL_Q, COL_K, COL_V, COL_G, COL_LR = 0, 1024, 2560, 2576, 3088, 3600, 4624, 5648
EPS = 1e-6
TINY = 1e-30
CREDIT = 4
TREE = [64, 32, 16, 8, 4, 2, 1]
LV = len(TREE) + 1
V_F1, V_MIX, V_F2, V_FIN, V_CW, V_CB, V_SN = 0, 16, 32, 48, 56, 104, 116
V_GN, V_HN, V_BG, V_LB = 128, 130, 131, 135
NV = 143
NORM_COL = [V_F1, V_MIX, V_F2, V_F1 + 8, V_MIX + 8, V_F2 + 8, V_FIN]
FIRST = 3


def dense_plan():
    phases, rows = [], []

    def phase(name, n, k):
        phases.append((name, len(rows), n, k))
        rows.extend([k] * n)

    def ffn(tag):
        for g, (_, nf) in enumerate(GROUPS):
            phase(f"{tag}_up{g}", 2 * nf, KT)
            phase(f"{tag}_down{g}", KT, nf)

    ffn("l0f1")
    phase("ab_small", 1, KT)
    phase("ab_xbc", NXT, KT)
    phase("ab_z", KT, KT)
    phase("ab_outy", KT, KT)
    phase("ab_heads", 16, KT)
    phase("ab_g", KT, KT)
    phase("ab_outo", KT, KT)
    ffn("l0f2")
    ffn("l1f1")
    phase("c_heads", 32, KT)
    phase("c_out", KT, KT)
    ffn("l1f2")
    return phases, rows


def build(nc, a, o):
    phases, unit_rows = dense_plan()
    plan = {name: (u, n, k) for name, u, n, k in phases}

    with ExitStack() as ctx:
        def sem(name):
            return ctx.enter_context(nc.semaphore(name))

        def at(name, shape, offset, dt=F):
            return nc.alloc_sbuf_tensor_at(name, [P] + list(shape), dt, offset=offset)

        def place(name, shape, where, dt=F):
            off, n = where[0], 4
            for s in shape:
                n *= s
            where[0] += (n + 63) // 64 * 64
            assert where[0] <= nc.sbuf_usable_end, (name, where[0], nc.sbuf_usable_end)
            return at(name, shape, off, dt)

        w = [(nc.sbuf_base + 63) // 64 * 64]
        H = place("H", [KT, T], w)
        XH = place("XH", [KT, T], w, FR)
        XL = place("XL", [KT, T], w, FR)
        raw = [place(f"raw{s}", [12, P], w) for s in range(4)]
        whi = [place(f"whi{s}", [12, P], w, FR) for s in range(2)]
        wlo = [place(f"wlo{s}", [12, P], w, FR) for s in range(2)]
        RS = place("RS", [T], w)
        LR = place("LR", [T], w)
        HSS = at("HSS", [D], w[0])
        SQ = place("SQ", [T], w)
        ACC = place("ACC", [T], w)
        assert 2 * T >= D
        ident = place("ident", [P], w)
        ones = place("ones", [P], w)
        vec = place("vec", [NV], w)
        cst = place("cst", [36], w)
        LB = place("LB", [4, KT], w)
        eps = place("eps", [1], w)
        free = w[0]

        w = [free]
        xin = place("xin", [NC + 1, D], w)
        rows = place("rows", [3, P], w)
        w = [free]
        YF = place("YF", [KT, TPAD], w)
        yout = place("yout", [2, D], w)
        w = [free]
        AH = place("AH", [12, T], w, FR)
        AL = place("AL", [12, T], w, FR)
        TG = place("TG", [T], w)
        TU = place("TU", [T], w)
        AV = place("AV", [T], w)
        w = [free]
        TRI = place("TRI", [P], w)
        DTG = place("DTG", [T], w)
        WGK = place("WGK", [512], w)
        keep_ab = w[0]
        XC = place("XC", [NXT, T], w)
        YH = at("YH", [KT, T], keep_ab, FR)
        keep_sz = w[0]
        SZ = place("SZ", [KT, T], w)
        YL = at("YL", [KT, T], keep_sz, FR)
        ssd0 = w[0]
        XE = [place(f"XE{b}", [T + 6], w) for b in range(2)]
        CV = [place(f"CV{b}", [T + 3], w) for b in range(2)]
        DTW = place("DTW", [8, T], w)
        XLAST = place("XLAST", [P], w)
        H0 = place("H0", [KT, P], w)
        conv_end = w[0]
        w = [ssd0]
        DC = LR
        XCC = place("XCC", [NXT, CH], w)
        DCC = place("DCC", [CH], w)
        DCT = place("DCT", [P], w)
        CE = place("CE", [HA], w)
        EE = place("EE", [HA], w)
        DE = place("DE", [HA], w)
        HIO = at("HIO", [KT, P], w[0])
        XD = place("XD", [D], w)
        HSIO = at("HSIO", [KT, P], w[0])
        XDE = place("XDE", [D], w)
        BT = place("BT", [2 * P], w)
        CBM = place("CBM", [2, CH], w)
        LM = place("LM", [4, 4, CH], w)
        EP = place("EP", [KT, CH], w)
        Y = place("Y", [KT, CH], w)
        RY = place("RY", [2, CH], w)
        assert w[0] >= conv_end
        CLST = place("CLST", [P], w)
        HS = place("HS", [D], w)
        DCOL = place("DCOL", [KT], w)
        D16 = place("D16", [1], w)
        SEL = place("SEL", [HA, P], w)
        SELP = place("SELP", [KT, P], w)

        def scan_memory(tag, start, nv):
            w = [start]
            m = {n: place(tag + n, s, w) for n, s in dict(
                st=[4, T], qw=[T], kw=[T], gw=[T], vw=[nv, TPAD], gs=[T], bw=[T], e1=[T], qe=[T], kd=[TPAD],
                xl=[LV - 1, T], vt=[NC + 1, nv * P], kt=[NC + 1, P], att=[NC, CH], ats=[TS], s=[NC + 1, nv * P],
                si=[nv * P], et=[NC + 1], rm=[T], mask=[5, P], wg=[P], o=[nv, T], sq=[nv, T]).items()}
            m["end"], m["nv"] = w[0], nv
            m["rh"], m["gn"] = LR, SQ
            return m

        GM = scan_memory("g_", keep_ab, 2)
        w = [GM["end"]]
        ON = place("ON", [KT, T], w)
        w = [keep_ab]
        GOH = place("GOH", [KT, T], w, FR)
        GOL = place("GOL", [KT, T], w, FR)
        GG = place("GG", [T], w)
        GS = place("GS", [T], w)
        assert w[0] <= GM["end"]
        CM = scan_memory("c_", free, 1)
        w = [CM["end"]]
        COH = place("COH", [KT, T], w, FR)
        COL = place("COL", [KT, T], w, FR)

        PD = ctx.enter_context(nc.psum_tensor("PD", [P, 4, 512], F))
        PM = ctx.enter_context(nc.psum_tensor("PM", [P, 4, 512], F))

        def pair(b):
            return PD[:, 2 * (b % 2):2 * (b % 2) + 2, 0:HT]

        def two(x):
            return x.rearrange("p (s t) -> p s t", s=2)

        def tile(x, m):
            return x[:, ds(m, 1), :].rearrange("p a t -> p (a t)")

        names = """hi_ready lo_ready unit_done pair_read consts_made rows_landed vec_psum vec_ready x_psum h_ready
            xh_ready xl_ready sq_ready acc_done ms_ready rs_ready gate_scaled silu_done act_made ah_ready al_ready
            lowrank_landed lb_in lb_exp small_landed ab_masks conv_ready xc_ready z_scaled sz_ready
            dt_abs dt_exp dt_plus dt_log last_rows last_psum last_copied last_stored d_psum selectors
            chunk_copied chunk_turned chunk_dct end_psum end_diff end_exp x_scaled cb_psum cb_masked
            cum_psum cum_diff decay_exp decay_made spread_psum spread_exp y_psum y_gated y_squared y_mean y_rstd
            y_weighted yh_ready yl_ready state_psum state_new h0_psum h0_landed h0_ready hout_psum hout_copied
            hout_stored scan_consts_made st_ready last_taken wg_copied gk_psum pre_act forget_made logs_made b_ready e1_ready
            kd_diff kd_exp kd_ready tree_diff tree_exp tree_made turned turned_read level_psum level_placed
            kv_psum s_ready o_psum o_copied o_mean o_rstd o_scaled oh_ready head_out s0_landed sp_stored ss_stored
            g_scaled gs_ready go_made goh_ready gol_ready y_ready yt_psum yt_copied yc_read""".split()
        S = {n: sem(n) for n in names}
        raw_landed = [sem(f"raw_landed{s}") for s in range(4)]
        x_landed = [sem(f"x_landed{s}") for s in range(2)]
        y_stored = [sem(f"y_stored{s}") for s in range(2)]
        passed = {e: sem(f"waits_passed_{e}") for e in ("sp", "act", "dve", "pe", "pool")}
        engines = {"sp": nc.sync, "act": nc.scalar, "dve": nc.vector, "pe": nc.tensor, "pool": nc.gpsimd}

        def hold(e, s, value):
            engines[e].wait_ge(s, value)
            if not isinstance(value, int):
                engines[e].sem_inc(passed[e], 1)

        def states_out(e):
            e.wait_ge(S["last_stored"], 32)
            e.wait_ge(S["hout_stored"], 64)

        def loop(e, lo, hi, body):
            if hi - lo >= 2:
                with engines[e].Fori(lo, hi) as i:
                    body(i)
            elif hi - lo == 1:
                body(lo)

        block = ctx.enter_context(nc.Block())

        @block.sync
        def _(sp):
            sp.wait_ge(S["consts_made"], 1)
            for col, name, pat, n in [
                    (V_F1, "norm_ffn1", "l (c p) -> (l c) p", 16), (V_MIX, "norm_mix", "l (c p) -> (l c) p", 16),
                    (V_F2, "norm_ffn2", "l (c p) -> (l c) p", 16), (V_FIN, "norm_final", "(c p) -> c p", 8),
                    (V_CW, "ssm_conv_w", "o k (c p) -> (o k c) p", 48), (V_CB, "ssm_conv_b", "o (c p) -> (o c) p", 12),
                    (V_SN, "ssm_norm_w", "o (c p) -> (o c) p", 8), (V_GN, "gla_norm_w", "o (c p) -> (o c) p", 2),
                    (V_HN, "hgrn_norm_w", "o (c p) -> (o c) p", 1), (V_BG, "gla_b_gk", "o (c p) -> (o c) p", 4),
                    (V_LB, "hgrn_lb_logits", "o (c p) -> (o c) p", 8), (2 * P, "state_conv", "o b r (c p) -> (o b r c) p", 36)]:
                sp.dma_start(rows[col % P:col % P + n, col // P, :], a[name].rearrange(pat, p=P)).then_inc(S["rows_landed"], 16)
            sp.dma_start(xin[:, 0:NC, :], a["x_prompt"].rearrange("b (c t) d -> t (b c) d", t=CH)).then_inc(x_landed[0], 16)
            sp.dma_start(xin[0:TS, NC, :], a["x_sample"].rearrange("b t d -> (b t) d")).then_inc(x_landed[1], 16)

            def load(u, slot, src, k, n=P, dst=0):
                hold("sp", S["lo_ready"], u + 1)
                return sp.dma_start(raw[slot][:, 0:k, dst:dst + n], src)

            def columns(name, view, start=0, end=None):
                u0, n, k = plan[name]

                def body(i):
                    for b in range(4):
                        s = (u0 + b) % 4
                        load(u0 + 4 * i + b, s, view(b, i), k).then_inc(raw_landed[s], 16)
                loop("sp", start, n // 4 if end is None else end, body)

            def ffn(tag, gu, down):
                gu = gu.rearrange("(k p) n -> p k n", p=P)
                for g, (f0, nf) in enumerate(GROUPS):
                    columns(f"{tag}_up{g}", lambda b, i: gu[:, :, ds(i * (2 * P) + ((b % 2) * FF + (f0 + b // 2) * P), P)])
                    dn = down[f0 * P:(f0 + nf) * P, :].rearrange("(k p) n -> p k n", p=P)
                    columns(f"{tag}_down{g}", lambda b, i: dn[:, :, ds(i * (4 * P) + b * P, P)])

            def plain(w, col):
                return lambda b, i: w[:, :, ds(i * (4 * P) + (col + b * P), P)]

            win = a["ab_w_in"][0].rearrange("(k p) n -> p k n", p=P)
            wy = a["ab_w_out"][0][0:D, :].rearrange("(k p) n -> p k n", p=P)
            wo = a["ab_w_out"][0][D:2 * D, :].rearrange("(k p) n -> p k n", p=P)
            cin = a["c_w_in"][0].rearrange("(k p) n -> p k n", p=P)
            cout = a["c_w_out"][0].rearrange("(k p) n -> p k n", p=P)

            ffn("l0f1", a["ffn1_w_gu"][0], a["ffn1_w_down"][0])
            u = plan["ab_small"][0]
            load(u, u % 4, win[:, :, COL_DT:COL_DT + HA], KT, HA, 0).then_inc(raw_landed[u % 4], 16)
            load(u, u % 4, win[:, :, COL_LR:COL_LR + 16], KT, 16, 32).then_inc(S["lowrank_landed"], 16)
            sp.wait_ge(S["h_ready"], 2 * KT)
            sp.dma_start(WGK[32:48, :], a["gla_w_gk"][0]).then_inc(S["small_landed"], 16)
            sp.dma_start(DTW[0:HA, 7, 0:1], a["ssm_dt_bias"].rearrange("o h -> h o")).then_inc(S["small_landed"], 16)
            sp.dma_start(DTW[0:HA, 7, 1:2], a["ssm_a_log"].rearrange("o h -> h o")).then_inc(S["small_landed"], 16)
            sp.dma_start(D16[32:48, 0:1], a["ssm_d"].rearrange("o h -> h o")).then_inc(S["small_landed"], 16)
            ssm = "o b (m e) p n -> (e p) (o b m) n"
            for e in range(2):
                sp.dma_start(H0[e * PA:(e + 1) * PA, :, :], a["state_ssm"].rearrange(ssm, e=2)[e * PA:(e + 1) * PA]).then_inc(S["h0_landed"], 16)
            columns("ab_xbc", plain(win, COL_XBC))
            columns("ab_z", plain(win, COL_Z))
            columns("ab_outy", plain(wy, 0), 0, 1)
            sp.wait_ge(S["last_copied"], 1)
            sp.dma_start(o["conv_p"].rearrange("o b r (c p) -> (o b r c) p", p=P), CLST[0:36, :]).then_inc(S["last_stored"], 16)
            sp.dma_start(o["conv_s"].rearrange("o b r (c p) -> (o b r c) p", p=P), CLST[36:72, :]).then_inc(S["last_stored"], 16)
            columns("ab_outy", plain(wy, 0), 1)
            for k, (dst, src) in enumerate(((o["ssm_p"], HIO), (o["ssm_s"], HSIO))):
                sp.wait_ge(S["hout_copied"], k + 1)
                for e in range(2):
                    sp.dma_start(dst.rearrange(ssm, e=2)[e * PA:(e + 1) * PA], src[e * PA:(e + 1) * PA, :, :]).then_inc(S["hout_stored"], 16)
            u0 = plan["ab_heads"][0]

            def gla(h):
                for b, col in enumerate([ds(h * P + COL_Q, P), ds(h * P + COL_K, P),
                                         ds(h * (2 * P) + COL_V, P), ds(h * (2 * P) + (COL_V + P), P)]):
                    s = (u0 + b) % 4
                    load(u0 + 4 * h + b, s, win[:, :, col], KT).then_inc(raw_landed[s], 16)
            loop("sp", 0, 4, gla)
            columns("ab_g", plain(win, COL_G))
            columns("ab_outo", plain(wo, 0))
            ffn("l0f2", a["ffn2_w_gu"][0], a["ffn2_w_down"][0])
            ffn("l1f1", a["ffn1_w_gu"][1], a["ffn1_w_down"][1])
            columns("c_heads", lambda b, h: cin[:, :, ds(h * P + b * D, P)])
            columns("c_out", plain(cout, 0))
            ffn("l1f2", a["ffn2_w_gu"][1], a["ffn2_w_down"][1])
            for c in range(NC + 1):
                sp.wait_ge(S["yt_copied"], c + 1)
                dst = o["y_p"][0, c * CH:(c + 1) * CH, :] if c < NC else o["y_s"][0]
                sp.dma_start(dst, yout[0:CH if c < NC else TS, c % 2, :]).then_inc(y_stored[c % 2], 16)
            sp.wait_ge(y_stored[0], 48)
            sp.wait_ge(y_stored[1], 32)
            sp.wait_ge(S["sp_stored"], 16 * 13)
            sp.wait_ge(S["ss_stored"], 16 * 13)

        @block.gpsimd
        def _(pool):
            pool.sem_inc(S["lo_ready"], CREDIT)
            pool.memset(rows[:, :, :], 0.0).then_inc(S["consts_made"], 1)
            pool.memset(ident[:, :], 0.0)
            pool.memset(ones[:, :], 1.0)
            pool.memset(eps[:, :], EPS)
            pool.drain()
            pool.affine_select(out=ident[:, :], in_=ident[:, :], compare_op=ALU.not_equal, fill=1.0, base=0,
                               pattern=[[-1, P]], channel_multiplier=1)
            pool.drain().then_inc(S["consts_made"], 1)

            def ab_masks():
                pool.wait_ge(S["h_ready"], 2 * KT)
                pool.memset(TRI[:, :], 1.0)
                pool.memset(XLAST[:, :], 0.0)
                pool.memset(XE[0][:, 0:3], 0.0)
                pool.memset(XE[1][:, 0:3], 0.0)
                pool.drain()
                pool.affine_select(out=TRI[:, :], in_=TRI[:, :], compare_op=ALU.is_ge, fill=0.0, base=0,
                                   pattern=[[1, P]], channel_multiplier=-1)
                pool.drain().then_inc(S["ab_masks"], 1)

            def selectors():
                pool.memset(SEL[:, :, :], 0.0)
                pool.memset(SELP[:, :, :], 0.0)
                pool.memset(HS[:, :], 0.0)
                pool.drain()
                pool.affine_select(out=SEL[:, :, :], in_=SEL[:, :, :], compare_op=ALU.not_equal, fill=1.0,
                                   base=-32, pattern=[[-1, HA], [0, P]], channel_multiplier=1)
                halves = SELP[:, :, :].rearrange("p m (e q) -> p m e q", e=2)
                pool.affine_select(out=halves, in_=halves, compare_op=ALU.not_equal, fill=1.0,
                                   base=-32, pattern=[[-2, KT], [-1, 2], [0, PA]], channel_multiplier=1)
                pool.drain().then_inc(S["selectors"], 1)

            def scan_consts(m):
                pool.memset(m["rm"][:, :], 1.0)
                pool.memset(m["mask"][:, :, :], 0.0)
                pool.memset(m["att"][:, :, :], 0.0)
                pool.memset(m["ats"][:, :], 0.0)
                pool.memset(m["vw"][:, :, T:TPAD], 0.0)
                pool.memset(m["kd"][:, T:TPAD], 0.0)
                pool.drain()
                pool.memset(m["rm"][:, 0:T:CH], 0.0)
                for n, hf in enumerate(TREE[2:]):
                    nodes = P // (2 * hf)
                    right = m["mask"][:, n, :].rearrange("p (b s r) -> p b s r", s=2, r=hf)[:, :, 1, :]
                    pool.memset(right, 1.0)
                    pool.drain()
                    pool.affine_select(out=right, in_=right, compare_op=ALU.is_ge, fill=0.0, base=0,
                                       pattern=[[-2 * hf, nodes], [0, hf]], channel_multiplier=1)
                    pool.drain()
                    pool.affine_select(out=right, in_=right, compare_op=ALU.is_ge, fill=0.0, base=hf - 1,
                                       pattern=[[2 * hf, nodes], [0, hf]], channel_multiplier=-1)
                pool.drain().then_inc(S["scan_consts_made"], 1)

            for name, u0, n, k in phases:
                if name == "ab_small":
                    ab_masks()
                if name == "ab_xbc":
                    selectors()
                if name == "ab_heads":
                    pool.wait_ge(S["unit_done"], u0 + CREDIT)
                    states_out(pool)
                    scan_consts(GM)
                if name == "c_heads":
                    pool.wait_ge(S["h_ready"], 5 * KT)
                    scan_consts(CM)

                def body(i):
                    for b in range(min(4, n)):
                        hold("pool", S["hi_ready"], u0 + 4 * i + (b + 1))
                        pool.tensor_tensor(wlo[(u0 + b) % 2][:, 0:k, :], raw[(u0 + b) % 4][:, 0:k, :],
                                           whi[(u0 + b) % 2][:, 0:k, :].bitcast(F), ALU.subtract).then_inc(S["lo_ready"], 1)
                loop("pool", 0, max(n // 4, 1), body)

        @block.scalar
        def _(act):
            A = act.activation

            def hi(ps, i, k):
                hold("act", raw_landed[ps % 4], 16 * i + 16 * (ps // 4 + 1))
                if ps == plan["ab_small"][0]:
                    act.wait_ge(S["lowrank_landed"], 16)
                hold("act", S["unit_done"], 4 * i + (ps - 1 + CREDIT))
                A(whi[ps % 2][:, 0:k, :], raw[ps % 4][:, 0:k, :], ACT.Copy).then_inc(S["hi_ready"], 1)

            def run(name, evac):
                u0, n, k = plan[name]
                steps = max(n // 4, 1)

                def body(i):
                    for b in range(min(4, n)):
                        hi(u0 + b + 2, i, k)
                        evac(i, b)
                loop("act", 0, steps - 1, body)
                i = steps - 1
                for b in range(min(4, n)):
                    ahead = u0 + 4 * i + b + 2
                    if ahead < len(unit_rows):
                        hi(ahead, 0, unit_rows[ahead])
                    evac(i, b)

            def x_out(e, m, final=False):
                hold("act", S["h_ready"], m + (e * KT + 1))
                if not final:
                    A(tile(XH, m), tile(H, m), ACT.Copy, scale=vec[:, ds(m + NORM_COL[e], 1)]).then_inc(S["xh_ready"], 1)
                hold("act", S["acc_done"], m + (9 * e + 1))
                A(SQ[:, :], tile(H, m), ACT.Square).then_inc(S["sq_ready"], 1)

            def rms(e):
                act.wait_ge(S["ms_ready"], e + 1)
                A(two(LR[:, :]), PM[:, 0:2, 0:HT], ACT.Ln, scale=1.0 / D, bias=eps[:, 0:1])
                act.drain()
                A(RS[:, :], LR[:, :], ACT.Exp, scale=-0.5).then_inc(S["rs_ready"], 1)

            hidden = [0]

            def ffn(tag, e, final=False):
                for g, (f0, nf) in enumerate(GROUPS):
                    base = hidden[0]

                    def up(i, b):
                        if b % 2 == 0:
                            hold("act", S["gate_scaled"], 2 * i + (base + b // 2 + 1))
                            A(TG[:, :], TG[:, :], ACT.Silu).then_inc(S["silu_done"], 1)
                        else:
                            hold("act", S["act_made"], 2 * i + (base + b // 2 + 1))
                            A(tile(AH, 2 * i + b // 2), AV[:, :], ACT.Copy).then_inc(S["ah_ready"], 1)
                    run(f"{tag}_up{g}", up)
                    hidden[0] += nf
                    run(f"{tag}_down{g}", (lambda i, b: x_out(e, 4 * i + b, final)) if g else (lambda i, b: None))
                rms(e)

            act.sem_inc(S["xc_ready"], 2)
            act.wait_ge(S["vec_psum"], 1)
            A(vec[:, 0:P], PM[:, 2, 0:P], ACT.Copy)
            A(vec[:, P:NV], PM[:, 2, P:NV], ACT.Copy)
            A(cst[:, :], PM[:, 2, 2 * P:2 * P + 36], ACT.Copy)
            act.drain().then_inc(S["vec_ready"], 1)
            act.wait_ge(S["lb_in"], 1)
            A(LB[:, 1, :], LB[:, 0, :], ACT.Exp).then_inc(S["lb_exp"], 1)
            for u in range(2):
                act.wait_ge(raw_landed[u], 16)
                A(whi[u][:, 0:KT, :], raw[u][:, 0:KT, :], ACT.Copy).then_inc(S["hi_ready"], 1)
            for m in range(KT):
                x_out(0, m)
            rms(0)
            ffn("l0f1", 1)

            run("ab_small", lambda i, b: None)

            def xbc(i, b):
                hold("act", S["conv_ready"], 4 * i + (b + 1))
                A(XC[:, ds(4 * i + b, 1), 0:TP].rearrange("p a t -> p (a t)"), CV[b % 2][:, 0:TP], ACT.Silu)
                A(XC[:, ds(4 * i + b, 1), TP:T].rearrange("p a t -> p (a t)"), CV[b % 2][:, TP + 3:T + 3], ACT.Silu)
                act.drain().then_inc(S["xc_ready"], 1)
            run("ab_xbc", xbc)

            def dt_exps():
                act.wait_ge(S["dt_abs"], 1)
                A(DTW[0:HA, 2, :], DTW[0:HA, 1, :], ACT.Exp, scale=-1.0)
                A(DTW[0:HA, 7, 2:3], DTW[0:HA, 7, 1:2], ACT.Exp)
                act.drain().then_inc(S["dt_exp"], 1)

            def dt_log():
                act.wait_ge(S["dt_plus"], 1)
                A(DTW[0:HA, 4, :], DTW[0:HA, 3, :], ACT.Ln).then_inc(S["dt_log"], 1)

            def small_copies():
                act.wait_ge(S["last_psum"], 1)
                A(CLST[:, :], PM[:, 2, 0:P], ACT.Copy).then_inc(S["last_copied"], 1)
                act.wait_ge(S["d_psum"], 1)
                A(DCOL[:, :], PM[:, 3, 0:KT], ACT.Copy)
                act.wait_ge(S["h0_psum"], 1)
                for b in range(2):
                    A(HSS[:, 512 * b:512 * b + 512], PM[:, b, :], ACT.Copy)
                act.drain().then_inc(S["h0_ready"], 1)

            def z(i, b):
                hold("act", S["z_scaled"], 4 * i + (b + 1))
                A(tile(SZ, 4 * i + b), tile(SZ, 4 * i + b), ACT.Silu).then_inc(S["sz_ready"], 1)
                {1: dt_exps, 2: small_copies, 3: dt_log}.get(4 * i + b, lambda: None)()
            run("ab_z", z)

            def copy_chunk(c, t0, n=CH):
                act.drain()
                hold("act", S["state_new"], c + 1)
                A(XCC[:, :, 0:n], XC[:, :, ds(t0, n)], ACT.Copy)
                A(DCC[:, 0:n], DC[:, ds(t0, n)], ACT.Copy)
                act.drain().then_inc(S["chunk_copied"], 1)

            def chunk_exps(c):
                hold("act", S["end_diff"], c + 1)
                A(EE[:, :], EE[:, :], ACT.Exp)
                A(DE[:, :], DE[:, :], ACT.Exp)
                act.drain().then_inc(S["end_exp"], 1)
                for q in range(4):
                    hold("act", S["cum_diff"], 4 * c + (q + 1))
                    A(LM[:, q], LM[:, q], ACT.Exp).then_inc(S["decay_exp"], 1)
                hold("act", S["spread_psum"], c + 1)
                for b in range(2):
                    A(EP[:, 4 * b:4 * b + 4, :].rearrange("p m t -> p (m t)"), PM[:, b, :], ACT.Exp)
                act.drain().then_inc(S["spread_exp"], 1)
                hold("act", S["y_gated"], c + 1)
                A(EP[:, :, :], Y[:, :, :], ACT.Square).then_inc(S["y_squared"], 1)

            def chunk_norm(c, t0, n=CH):
                hold("act", S["y_mean"], c + 1)
                ry = RY[:, :, :].rearrange("p g t -> p (g t)")
                A(ry, PM[:, 3, 2 * CH:4 * CH], ACT.Ln, scale=2.0 / D, bias=eps[:, 0:1])
                act.drain()
                A(ry, ry, ACT.Exp, scale=-0.5).then_inc(S["y_rstd"], 1)
                hold("act", S["y_weighted"], c + 1)
                A(YH[:, :, ds(t0, n)], Y[:, :, 0:n], ACT.Copy).then_inc(S["yh_ready"], 1)

            def state_rows(k, dst):
                act.wait_ge(S["hout_psum"], k + 1)
                for b in range(2):
                    A(dst[:, 4 * b:4 * b + 4, :].rearrange("p m n -> p (m n)"), PM[:, 2 * k + b, :], ACT.Copy)
                act.drain().then_inc(S["hout_copied"], 1)

            act.sem_inc(S["y_rstd"], 1)
            copy_chunk(0, 0)
            with act.Fori(0, NC - 1) as c:
                chunk_exps(c)
                copy_chunk(c + 1, c * CH + CH)
                chunk_norm(c, c * CH)
            chunk_exps(NC - 1)
            copy_chunk(NC, TP, TS)
            chunk_norm(NC - 1, TP - CH)
            chunk_exps(NC)
            chunk_norm(NC, TP, TS)
            state_rows(0, HIO)
            run("ab_outy", lambda i, b: state_rows(1, HSIO) if 4 * i + b == 0 else None)

            def heads(name, nh, m, g0, scale, t0):
                u0 = plan[name][0]
                nv = m["nv"]
                gla = nv == 2

                def scan(j):
                    g = j + g0
                    st = m["st"]

                    def load_state():
                        src = (a["state_gla"] if gla else a["state_hgrn"])[0, 0]
                        act.dma_start(m["si"][:, :], src[ds(j, 1), :, :].rearrange("h k v -> k (h v)")).then_inc(S["s0_landed"], 16)

                    def take():
                        hold("act", S["st_ready"], 4 * g + 3)
                        if gla:
                            A(m["wg"][32:48, :], WGK[32:48, ds(j * P, P)], ACT.Copy).then_inc(S["wg_copied"], 1)
                            A(m["qw"][:, :], st[:, 0, :], ACT.Copy, scale=float(P) ** -0.5)
                            A(m["kw"][:, :], st[:, 1, :], ACT.Copy)
                            A(m["vw"][:, 0, 0:T], st[:, 2, :], ACT.Copy)
                        else:
                            A(m["qw"][:, :], st[:, 0, :], ACT.Sigmoid)
                            A(m["kw"][:, :], st[:, 1, :], ACT.Sigmoid)
                            A(m["vw"][:, 0, 0:T], st[:, 2, :], ACT.Copy)
                            act.drain().then_inc(S["pre_act"], 1)

                    def forget():
                        if not gla:
                            hold("act", S["forget_made"], j + 1)
                            A(m["bw"][:, :], m["bw"][:, :], ACT.Ln)
                            A(m["e1"][:, :], m["e1"][:, :], ACT.Ln)
                            act.drain().then_inc(S["logs_made"], 1)

                    def gate_logits():
                        if gla:
                            hold("act", S["gk_psum"], g + 1)
                            bias = vec[:, ds(j + V_BG, 1)]
                            A(two(m["gw"][:, :]), PM[:, 0:2, 0:HT], ACT.Identity, bias=bias)
                            A(two(m["e1"][:, :]), PM[:, 0:2, 0:HT], ACT.Abs, bias=bias)
                            act.drain()
                            A(m["e1"][:, :], m["e1"][:, :], ACT.Exp, scale=-1.0)
                            act.drain()
                            A(m["e1"][:, :], m["e1"][:, :], ACT.Ln, bias=1.0)
                            act.drain().then_inc(S["pre_act"], 1)

                    def decay():
                        hold("act", S["b_ready"], g + 1)
                        A(m["e1"][:, :], m["bw"][:, :], ACT.Exp, scale=scale).then_inc(S["e1_ready"], 1)
                        hold("act", S["kd_diff"], g + 1)
                        A(m["kd"][:, 0:T], m["kd"][:, 0:T], ACT.Exp, scale=scale).then_inc(S["kd_exp"], 1)

                    def exps(lo, up):
                        for n in range(lo, up):
                            hold("act", S["tree_diff"], (LV - 1) * g + (n + 1))
                            t = TP if n < 2 else T
                            A(m["xl"][:, n, 0:t], m["xl"][:, n, 0:t], ACT.Exp, scale=scale).then_inc(S["tree_exp"], 1)

                    def take_last():
                        hold("act", S["st_ready"], 4 * g + 4)
                        if gla:
                            A(m["vw"][:, 1, 0:T], st[:, 3, :], ACT.Copy).then_inc(S["last_taken"], 1)
                        else:
                            A(m["gn"][:, :], st[:, 3, :], ACT.Sigmoid).then_inc(S["last_taken"], 1)

                    def turned():
                        for v in range(nv + 1):
                            hold("act", S["turned"], (nv + 1) * j + (t0 + v + 1))
                            dst = m["vt"][:, :, v * P:(v + 1) * P] if v < nv else m["kt"][:, :, :]
                            b = 2 * (v % 2)
                            A(dst[:, 0:NC, :], PM[:, b, :].rearrange("p (c k) -> p c k", c=NC), ACT.Copy)
                            A(dst[:, NC, :], PM[:, b + 1, 0:P], ACT.Copy)
                            act.drain().then_inc(S["turned_read"], 1)

                    def levels_done():
                        hold("act", S["level_placed"], LV * g + LV)

                    def copy_out():
                        hold("act", S["o_psum"], g + 1)
                        hold("act", S["head_out"], g + 1)
                        for v in range(nv):
                            for dst, f in ((m["o"], ACT.Copy), (m["sq"], ACT.Square)):
                                A(dst[:, v, 0:TP], PM[:, v, :], f)
                                A(dst[:, v, TP:T], PM[:, 2, v * TS:(v + 1) * TS], f)
                        act.drain().then_inc(S["o_copied"], 1)

                    def store_states():
                        pre_ = "gla" if gla else "hgrn"
                        act.dma_start(o[pre_ + "_p"][0, 0][ds(j, 1), :, :].rearrange("h k v -> k (h v)"), m["s"][:, NC - 1, :]).then_inc(S["sp_stored"], 16)
                        act.dma_start(o[pre_ + "_s"][0, 0][ds(j, 1), :, :].rearrange("h k v -> k (h v)"), m["s"][:, NC, :]).then_inc(S["ss_stored"], 16)

                    def rstd():
                        hold("act", S["o_mean"], g + 1)
                        A(two(m["rh"][:, :]), PM[:, 2:4, 0:HT], ACT.Ln, scale=1.0 / (nv * P), bias=eps[:, 0:1])
                        act.drain()
                        A(m["rh"][:, :], m["rh"][:, :], ACT.Exp, scale=-0.5).then_inc(S["o_rstd"], 1)

                    def out_hi():
                        if not gla:
                            hold("act", S["o_scaled"], j + 1)
                            A(tile(COH, j), m["o"][:, 0, :], ACT.Copy).then_inc(S["oh_ready"], 1)
                    return dict(load_state=load_state, take=take, forget=forget, gate_logits=gate_logits, decay=decay,
                                exps=exps, take_last=take_last, turned=turned, levels_done=levels_done, copy_out=copy_out,
                                store_states=store_states, rstd=rstd, out_hi=out_hi)

                for b in range(4):
                    hi(u0 + b + 2, 0, KT)
                new = scan(0)
                for part in ("load_state", "take", "forget", "gate_logits", "decay"):
                    new[part]()
                new["exps"](0, FIRST)

                def body(h):
                    old, new = scan(h - 1), scan(h)
                    hi(u0 + 2, h, KT)
                    old["exps"](FIRST, LV - 1)
                    old["take_last"]()
                    hi(u0 + 3, h, KT)
                    hi(u0 + 4, h, KT)
                    old["turned"]()
                    old["levels_done"]()
                    new["take"]()
                    new["forget"]()
                    old["copy_out"]()
                    new["gate_logits"]()
                    new["decay"]()
                    hi(u0 + 5, h, KT)
                    old["rstd"]()
                    new["exps"](0, FIRST)
                    old["out_hi"]()
                    old["store_states"]()
                    new["load_state"]()
                loop("act", 1, nh, body)
                old = scan(nh - 1)
                old["exps"](FIRST, LV - 1)
                for part in ("take_last", "turned", "copy_out", "rstd", "out_hi", "store_states"):
                    old[part]()

            states_out(act)
            act.sem_inc(S["sp_stored"], 16)
            act.sem_inc(S["ss_stored"], 16)
            heads("ab_heads", 4, GM, 0, 1.0 / 16.0, 0)

            def gate(i, b):
                hold("act", S["g_scaled"], 4 * i + (b + 1))
                A(GS[:, :], GG[:, :], ACT.Silu).then_inc(S["gs_ready"], 1)
                hold("act", S["go_made"], 4 * i + (b + 1))
                A(tile(GOH, 4 * i + b), GG[:, :], ACT.Copy).then_inc(S["goh_ready"], 1)
            run("ab_g", gate)
            run("ab_outo", lambda i, b: x_out(2, 4 * i + b))
            rms(2)
            ffn("l0f2", 3)
            ffn("l1f1", 4)
            heads("c_heads", 8, CM, 4, 1.0, 12)
            run("c_out", lambda i, b: x_out(5, 4 * i + b))
            rms(5)
            ffn("l1f2", 6, final=True)
            for c in range(NC + 1):
                act.wait_ge(S["yt_psum"], c + 1)
                if c >= 2:
                    act.wait_ge(y_stored[c % 2], 16 * (c // 2))
                A(yout[:, c % 2, :], PM[:, 2 * (c % 2):2 * (c % 2) + 2, :].rearrange("p s t -> p (s t)"), ACT.Copy).then_inc(S["yt_copied"], 1)

        @block.vector
        def _(dve):
            TT, STT, TSC = dve.tensor_tensor, dve.scalar_tensor_tensor, dve.tensor_scalar

            def run(name, evac):
                u0, n, _ = plan[name]

                def body(i):
                    for b in range(min(2, n)):
                        hold("dve", S["unit_done"], 2 * i + (u0 + b + 1 + CREDIT))
                        evac(2 * i + b, u0 + b, b)
                loop("dve", 0, max(n // 2, 1), body)

            def x_out(e, m, final=False):
                if not final:
                    hold("dve", S["xh_ready"], m + (e * KT + 1))
                    STT(tile(XL, m), tile(H, m), vec[:, ds(m + NORM_COL[e], 1)], tile(XH, m).bitcast(F),
                        ALU.mult, ALU.subtract).then_inc(S["xl_ready"], 1)
                hold("dve", S["sq_ready"], m + (e * KT + 1))
                TT(ACC[:, :], ACC[:, :], SQ[:, :], ALU.add)
                dve.drain().then_inc(S["acc_done"], 1)

            def clear_acc():
                dve.memset(ACC[:, :], 0.0)
                dve.drain().then_inc(S["acc_done"], 1)

            def residual(e, scale, with_x, final=False):
                def evac(m, ps, b):
                    STT(two(tile(H, m)), pair(ps), scale, two(tile(H, m)), ALU.mult, ALU.add)
                    dve.drain().then_inc(S["pair_read"], 1)
                    if with_x:
                        dve.sem_inc(S["h_ready"], 1)
                        x_out(e, m, final)
                return evac

            hidden = [0]

            def ffn(tag, e, final=False):
                dve.wait_ge(S["rs_ready"], e)
                for g, (f0, nf) in enumerate(GROUPS):
                    base = hidden[0]

                    def up(u, ps, b):
                        if b == 0:
                            TT(two(TG[:, :]), pair(ps), two(RS[:, :]), ALU.mult).then_inc(S["gate_scaled"], 1)
                            dve.drain().then_inc(S["pair_read"], 1)
                            return
                        TT(two(TU[:, :]), pair(ps), two(RS[:, :]), ALU.mult)
                        dve.drain().then_inc(S["pair_read"], 1)
                    u0, n, _ = plan[f"{tag}_up{g}"]

                    def body(i):
                        for b in range(2):
                            hold("dve", S["unit_done"], 2 * i + (u0 + b + 1 + CREDIT))
                            up(None, u0 + b, b)
                        hold("dve", S["silu_done"], i + (base + 1))
                        TT(AV[:, :], TG[:, :], TU[:, :], ALU.mult).then_inc(S["act_made"], 1)
                        dve.drain()
                        hold("dve", S["ah_ready"], i + (base + 1))
                        TT(tile(AL, i), AV[:, :], tile(AH, i).bitcast(F), ALU.subtract).then_inc(S["al_ready"], 1)
                        dve.drain()
                    loop("dve", 0, nf, body)
                    hidden[0] += nf
                    if g:
                        clear_acc()
                    run(f"{tag}_down{g}", residual(e, 0.5, g == 1, final))

            dve.sem_inc(S["pair_read"], CREDIT)
            dve.wait_ge(S["vec_ready"], 1)
            TT(LB[:, 0, :], vec[:, V_LB:V_LB + KT], vec[:, V_LB:V_LB + KT], ALU.subtract).then_inc(S["lb_in"], 1)
            dve.wait_ge(S["lb_exp"], 1)
            dve.reciprocal(LB[:, 2, :], LB[:, 1, :])
            dve.drain()
            TT(LB[:, 1, :], LB[:, 1, :], LB[:, 2, :], ALU.mult)
            dve.drain()
            TT(LB[:, 2, :], LB[:, 1, :], LB[:, 1, :], ALU.subtract)
            dve.drain()
            TSC(LB[:, 3, :], LB[:, 2, :], -1.0, 1.0, ALU.mult, ALU.add)
            clear_acc()
            for m in range(KT):
                dve.wait_ge(S["x_psum"], m + 1)
                b = 2 * (m % 2)
                dve.tensor_copy(H[:, m, 0:TP], PM[:, b, :])
                dve.tensor_copy(H[:, m, TP:T], PM[:, b + 1, 0:TS])
                dve.drain().then_inc(S["h_ready"], 1)
                x_out(0, m)
            ffn("l0f1", 1)

            dve.wait_ge(S["rs_ready"], 2)

            def small(m, ps, b):
                TT(two(DTG[0:64, :]), pair(ps)[0:64], two(RS[0:64, :]), ALU.mult)
                dve.drain().then_inc(S["pair_read"], 1)
            run("ab_small", small)
            dve.wait_ge(S["ab_masks"], 1)

            def xbc(m, ps, b):
                e, cv, s0, s1 = XE[b], CV[b], PD[:, 2 * (ps % 2), :], PD[:, 2 * (ps % 2) + 1, :]
                TT(e[:, 3:3 + HT], s0[:, 0:HT], RS[:, 0:HT], ALU.mult)
                TT(e[:, 3 + HT:3 + TP], s1[:, 0:TP - HT], RS[:, HT:TP], ALU.mult)
                TT(e[:, TP + 6:T + 6], s1[:, TP - HT:HT], RS[:, TP:T], ALU.mult)
                dve.tensor_copy(e[:, TP + 3:TP + 6], cst[:, :].rearrange("p (r c) -> p c r", r=3)[:, ds(m, 1), :].rearrange("p a r -> p (a r)"))
                dve.drain().then_inc(S["pair_read"], 1)
                hold("dve", S["xc_ready"], m + 1)
                TSC(cv[:, :], e[:, 0:T + 3], vec[:, ds(m + V_CW, 1)], vec[:, ds(m + V_CB, 1)], ALU.mult, ALU.add)
                for k in range(1, 4):
                    dve.drain()
                    last = STT(cv[:, :], e[:, k:k + T + 3], vec[:, ds(m + (V_CW + NXT * k), 1)], cv[:, :], ALU.mult, ALU.add)
                last.then_inc(S["conv_ready"], 1)
                keep = XLAST[:, 0:6 * NXT].rearrange("p (r c) -> p c r", r=6)[:, ds(m, 1), :].rearrange("p a r -> p (a r)")
                dve.tensor_copy(keep[:, 0:3], e[:, TP:TP + 3])
                dve.tensor_copy(keep[:, 3:6], e[:, T + 3:T + 6])
                dve.drain()
            run("ab_xbc", xbc)
            dve.sem_inc(S["last_rows"], 1)

            def z(m, ps, b):
                TT(two(tile(SZ, m)), pair(ps), two(RS[:, :]), ALU.mult).then_inc(S["z_scaled"], 1)
                dve.drain().then_inc(S["pair_read"], 1)

            d = [DTW[0:HA, n, :] for n in range(7)]

            def dt_abs():
                dve.wait_ge(S["small_landed"], 64)
                TSC(d[0], DTG[0:HA, :], DTW[0:HA, 7, 0:1], None, ALU.add)
                dve.drain()
                STT(d[1], d[0], -1.0, d[0], ALU.mult, ALU.max).then_inc(S["dt_abs"], 1)

            def dt_plus():
                dve.wait_ge(S["dt_exp"], 1)
                TSC(d[3], d[2], 1.0, None, ALU.add).then_inc(S["dt_plus"], 1)
                dve.drain()
                TSC(d[5], d[3], -1.0, None, ALU.add)
                dve.drain()
                TSC(d[6], d[5], 0.0, None, ALU.is_equal)
                dve.drain()
                TT(d[5], d[5], d[6], ALU.add)
                dve.drain()

            def dt_divide():
                dve.reciprocal(d[5], d[5])
                dve.drain()

            def dt_softplus():
                dve.wait_ge(S["dt_log"], 1)
                TT(d[4], d[4], d[6], ALU.add)
                dve.drain()
                TT(d[4], d[4], d[2], ALU.mult)
                dve.drain()
                TT(d[4], d[4], d[5], ALU.mult)
                dve.drain()
                STT(d[4], d[0], 0.0, d[4], ALU.max, ALU.add)
                dve.drain()

            def dt_cumulated():
                TSC(d[5], d[4], DTW[0:HA, 7, 2:3], -1.0, ALU.mult, ALU.mult)
                dve.memset(d[6], 1.0)
                dve.drain()
                dve.memset(d[6][:, 0:T:CH], 0.0)
                dve.drain()
                dve.tensor_tensor_scan(d[3], d[6], d[5], 0.0, ALU.mult, ALU.add)
                dve.drain()

            def dt_place():
                dve.memset(DC[:, :], 0.0)
                dve.drain()
                dve.tensor_copy(DC[0:HA, :], d[4])
                dve.tensor_copy(DC[32:32 + HA, :], d[3])
                dve.drain()

            between = {0: dt_abs, 2: dt_plus, 3: dt_divide, 4: dt_softplus, 5: dt_cumulated, 6: dt_place}
            u0 = plan["ab_z"][0]
            for m in range(KT):
                dve.wait_ge(S["unit_done"], u0 + m + 1 + CREDIT)
                z(m, u0 + m, m)
                if m in between:
                    between[m]()
            dve.wait_ge(S["sz_ready"], KT)
            dve.wait_ge(S["h0_ready"], 1)
            dve.sem_inc(S["yl_ready"], 1)
            dve.sem_inc(S["state_new"], 1)

            def heads_over(x, n):
                return x.unsqueeze(2).broadcast_to([P, x.shape[1], n])

            def chunk_columns(c, n=CH):
                hold("dve", S["chunk_turned"], c + 1)
                dve.tensor_copy(DCT[:, :], PM[:, 2, 2 * P:3 * P])
                dve.tensor_copy(BT[:, :], PM[:, 2, 0:2 * P])
                TSC(CE[32:48, :], ident[32:48, 32:48], DCC[32:48, n - 1:n], None, ALU.mult)
                dve.drain().then_inc(S["chunk_dct"], 1)

            def chunk_body(c, t0, n=CH, before=None, state=HS):
                hold("dve", S["end_psum"], c + 1)
                dve.tensor_copy(EE[:, :], PM[:, 2, 384:384 + HA])
                TT(DE[:, :], PM[:, 2, 384:384 + HA], DCT[:, 32:48], ALU.subtract)
                dve.drain()
                TSC(DE[:, :], DE[:, :], 0.0, None, ALU.min)
                dve.drain().then_inc(S["end_diff"], 1)
                xd = XD[:, :].rearrange("p (h q) -> p h q", q=PA)
                TT(xd, PM[:, 0:2, :].rearrange("p s (h q) -> p (s h) q", q=PA), heads_over(DCT[:, 0:HA], PA), ALU.mult)
                dve.drain()
                if before is not None:
                    chunk_lo(*before)
                hold("dve", S["end_exp"], c + 1)
                TT(XDE[:, :].rearrange("p (h q) -> p h q", q=PA), xd, heads_over(DE[:, :], PA), ALU.mult)
                dve.drain().then_inc(S["x_scaled"], 1)
                hold("dve", S["cb_psum"], c + 1)
                TT(CBM[:, :, :], PM[:, 3, 0:2 * CH].rearrange("p (g t) -> p g t", g=2),
                   TRI[:, :].unsqueeze(1).broadcast_to([P, 2, CH]), ALU.mult).then_inc(S["cb_masked"], 1)
                for q in range(4):
                    hold("dve", S["cum_psum"], 4 * c + (q + 1))
                    TT(LM[:, q], PD[:, q, :].rearrange("p (h t) -> p h t", h=4), heads_over(DCT[:, 32 + 4 * q:36 + 4 * q], CH), ALU.subtract)
                    dve.drain()
                    TSC(LM[:, q], LM[:, q], 0.0, None, ALU.min).then_inc(S["cum_diff"], 1)
                for q in range(4):
                    hold("dve", S["decay_exp"], 4 * c + (q + 1))
                    TT(LM[:, q], LM[:, q], CBM[:, q // 2, :].unsqueeze(1).broadcast_to([P, 4, CH]), ALU.mult).then_inc(S["decay_made"], 1)
                hold("dve", S["y_psum"], c + 1)
                hold("dve", S["spread_exp"], c + 1)
                TT(Y[:, :, :], PD[:, 2:4, :].rearrange("p s (m t) -> p (s m) t", t=CH), EP[:, :, :], ALU.mult)
                dve.drain()
                TT(Y[:, :, :], PD[:, 0:2, :].rearrange("p s (m t) -> p (s m) t", t=CH), Y[:, :, :], ALU.add)
                dve.drain()
                for m in range(KT):
                    STT(Y[:, m, :], XCC[:, m, :], DCOL[:, m:m + 1], Y[:, m, :], ALU.mult, ALU.add)
                dve.drain()
                TT(Y[:, :, 0:n], Y[:, :, 0:n], SZ[:, :, ds(t0, n)], ALU.mult)
                dve.drain().then_inc(S["y_gated"], 1)
                hold("dve", S["state_psum"], c + 1)
                hs = state[:, :].rearrange("p (h q) -> p h q", q=PA)
                TT(hs, hs, heads_over(EE[:, :], PA), ALU.mult)
                dve.drain()
                TT(state[:, :], PM[:, 0:2, :].rearrange("p s t -> p (s t)"), state[:, :], ALU.add)
                dve.drain().then_inc(S["state_new"], 1)

            def chunk_norm(c):
                hold("dve", S["y_rstd"], c + 2)
                for g in range(2):
                    TT(Y[:, 4 * g:4 * g + 4, :], Y[:, 4 * g:4 * g + 4, :], RY[:, g, :].unsqueeze(1).broadcast_to([P, 4, CH]), ALU.mult)
                dve.drain()
                TT(Y[:, :, :], Y[:, :, :], heads_over(vec[:, V_SN:V_SN + KT], CH), ALU.mult)
                dve.drain().then_inc(S["y_weighted"], 1)

            def chunk_lo(c, t0, n=CH):
                hold("dve", S["yh_ready"], c + 1)
                TT(YL[:, :, ds(t0, n)], Y[:, :, 0:n], YH[:, :, ds(t0, n)].bitcast(F), ALU.subtract).then_inc(S["yl_ready"], 1)

            chunk_columns(0)
            chunk_body(0, 0)
            with dve.Fori(1, NC) as c:
                chunk_columns(c)
                chunk_norm(c - 1)
                chunk_body(c, c * CH, before=(c - 1, c * CH - CH))
            chunk_columns(NC, TS)
            chunk_norm(NC - 1)
            chunk_body(NC, TP, TS, before=(NC - 1, TP - CH), state=HSS)
            chunk_norm(NC)
            chunk_lo(NC, TP, TS)
            run("ab_outy", residual(1, 1.0, False))

            def heads(name, nh, m, g0, weights, first):
                u0 = plan[name][0]
                nv = m["nv"]
                gla = nv == 2
                b_, q_, k_ = m["bw"], m["qw"], m["kw"]

                def units(h, b):
                    hold("dve", S["unit_done"], 4 * h + (u0 + b + 1 + CREDIT))
                    TT(two(m["st"][:, b, :]), pair(u0 + b), two(RS[:, :]), ALU.mult).then_inc(S["st_ready"], 1)
                    dve.drain().then_inc(S["pair_read"], 1)

                def scan(j):
                    g = j + g0

                    def pre():
                        hold("dve", S["pre_act"], g + 1)
                        if gla:
                            STT(m["gw"][:, :], m["gw"][:, :], 0.0, m["e1"][:, :], ALU.min, ALU.subtract)
                        else:
                            TT(q_[:, :], q_[:, :], m["st"][:, 0, :], ALU.mult)
                            TSC(m["gw"][:, :], k_[:, :], LB[:, 3, ds(j, 1)], LB[:, 2, ds(j, 1)], ALU.mult, ALU.add)
                            dve.drain()
                            TSC(b_[:, :], m["gw"][:, :], 2.0 ** -60, None, ALU.max)
                            TSC(m["e1"][:, :], m["gw"][:, :], TINY, 2.0 ** 60, ALU.max, ALU.mult)
                            dve.drain()
                            TSC(m["e1"][:, :], m["e1"][:, :], 1.0, None, ALU.min)
                            TSC(k_[:, :], m["gw"][:, :], -1.0, 1.0, ALU.mult, ALU.add)
                            dve.drain().then_inc(S["forget_made"], 1)
                            hold("dve", S["logs_made"], j + 1)
                            TT(m["gw"][:, :], b_[:, :], m["e1"][:, :], ALU.add)
                        dve.drain()
                        dve.tensor_tensor_scan(b_[:, :], m["rm"][:, :], m["gw"][:, :], 0.0, ALU.mult, ALU.add).then_inc(S["b_ready"], 1)
                        dve.drain()

                    def end_diffs():
                        bc = b_[:, 0:TP].rearrange("p (c t) -> p c t", c=NC)
                        TT(m["kd"][:, 0:TP].rearrange("p (c t) -> p c t", c=NC), bc[:, :, CH - 1:CH].broadcast_to([P, NC, CH]), bc, ALU.subtract)
                        TT(m["kd"][:, TP:T], b_[:, T - 1:T].broadcast_to([P, TS]), b_[:, TP:T], ALU.subtract)
                        dve.drain().then_inc(S["kd_diff"], 1)

                    def diffs(lo, up):
                        for n in range(lo, up):
                            hf = TREE[n]
                            t = TP if n < 2 else T
                            bn = b_[:, 0:t].rearrange("p (n s r) -> p n s r", s=2, r=hf)
                            xn = m["xl"][:, n, 0:t].rearrange("p (n s r) -> p n s r", s=2, r=hf)
                            mid = bn[:, :, 0, hf - 1:hf].broadcast_to([P, t // (2 * hf), hf])
                            TT(xn[:, :, 0, :], mid, bn[:, :, 0, :], ALU.subtract)
                            TT(xn[:, :, 1, :], bn[:, :, 1, :], mid, ALU.subtract)
                            dve.drain().then_inc(S["tree_diff"], 1)

                    def decayed():
                        hold("dve", S["e1_ready"], g + 1)
                        TT(m["qe"][:, :], m["e1"][:, :], q_[:, :], ALU.mult)
                        dve.tensor_copy(m["et"][:, 0:NC], m["e1"][:, CH - 1:TP:CH])
                        dve.tensor_copy(m["et"][:, NC:NC + 1], m["e1"][:, T - 1:T])
                        hold("dve", S["kd_exp"], g + 1)
                        TT(m["kd"][:, 0:T], m["kd"][:, 0:T], k_[:, :], ALU.mult)
                        dve.drain().then_inc(S["kd_ready"], 1)

                    def products():
                        for n, hf in enumerate(TREE):
                            t = TP if n < 2 else T
                            hold("dve", S["tree_exp"], (LV - 1) * g + (n + 1))
                            xn = m["xl"][:, n, 0:t].rearrange("p (n s r) -> p n s r", s=2, r=hf)
                            for s, y in ((0, k_), (1, q_)):
                                yn = y[:, 0:t].rearrange("p (n s r) -> p n s r", s=2, r=hf)
                                TT(xn[:, :, s, :], xn[:, :, s, :], yn[:, :, s, :], ALU.mult)
                            dve.drain().then_inc(S["tree_made"], 1)
                        if not gla:
                            hold("dve", S["last_taken"], g + 1)
                            TT(m["gs"][:, :], m["gn"][:, :], m["st"][:, 3, :], ALU.mult)
                            dve.drain()

                    def levels():
                        for n in range(LV):
                            hold("dve", S["level_psum"], LV * g + (n + 1))
                            src = PM[:, n % 2, :].rearrange("p (c t) -> p c t", c=NC)
                            if n == 0:
                                dve.tensor_copy(m["att"][0:64, :, 64:128], src[0:64, :, 64:128])
                            elif n == 1:
                                for e in range(2):
                                    dve.tensor_copy(m["att"][64 * e:64 * e + 32, :, 64 * e + 32:64 * e + 64],
                                                    src[64 * e:64 * e + 32, :, 64 * e + 32:64 * e + 64])
                            else:
                                mk = m["mask"][:, n - 2, :] if n < LV - 1 else ident[:, :]
                                dve.copy_predicated(m["att"][:, :, :], mk.bitcast(I32).unsqueeze(1).broadcast_to([P, NC, CH]), src)
                                dve.copy_predicated(m["ats"][0:TS, :], mk[0:TS, 0:TS].bitcast(I32), PM[0:TS, 2 + n % 2, 0:TS])
                            dve.drain().then_inc(S["level_placed"], 1)

                    def states():
                        hold("dve", S["kv_psum"], g + 1)
                        hold("dve", S["s0_landed"], 16 * g + 16)
                        hold("dve", S["sp_stored"], 16 * g + 16)
                        hold("dve", S["ss_stored"], 16 * g + 16)
                        per = 4 // nv

                        def kv(c):
                            return PM[:, c // per, (c % per) * nv * P:(c % per + 1) * nv * P]
                        dve.tensor_copy(m["s"][:, 0, :], kv(0))
                        STT(m["s"][:, NC, :], m["si"][:, :], m["et"][:, NC:NC + 1], kv(NC), ALU.mult, ALU.add)
                        for c in range(1, NC):
                            dve.drain()
                            STT(m["s"][:, c, :], m["s"][:, c - 1, :], m["et"][:, c:c + 1], kv(c), ALU.mult, ALU.add)
                        dve.drain().then_inc(S["s_ready"], 1)

                    def out():
                        hold("dve", S["o_rstd"], g + 1)
                        for v in range(nv):
                            dst = tile(ON, 2 * j + v) if gla else m["o"][:, v, :]
                            STT(dst, m["o"][:, v, :], vec[:, weights + v:weights + v + 1], m["rh"][:, :], ALU.mult, ALU.mult)
                        if gla:
                            dve.drain().then_inc(S["head_out"], 1)
                            return
                        dve.drain()
                        TT(m["o"][:, 0, :], m["o"][:, 0, :], m["gs"][:, :], ALU.mult).then_inc(S["o_scaled"], 1)
                        dve.drain()

                    def out_lo():
                        if not gla:
                            hold("dve", S["oh_ready"], j + 1)
                            TT(tile(COL, j), m["o"][:, 0, :], tile(COH, j).bitcast(F), ALU.subtract)
                            dve.drain().then_inc(S["head_out"], 1)
                    return dict(pre=pre, end_diffs=end_diffs, diffs=diffs, decayed=decayed, products=products, levels=levels,
                                states=states, out=out, out_lo=out_lo)

                dve.wait_ge(S["scan_consts_made"], first)
                for b in range(4):
                    units(0, b)
                new = scan(0)
                new["pre"]()
                new["end_diffs"]()
                new["diffs"](0, FIRST)

                def body(h):
                    old, new = scan(h - 1), scan(h)
                    units(h, 0)
                    old["diffs"](FIRST, LV - 1)
                    old["decayed"]()
                    units(h, 1)
                    old["products"]()
                    units(h, 2)
                    old["levels"]()
                    old["states"]()
                    new["pre"]()
                    new["end_diffs"]()
                    units(h, 3)
                    new["diffs"](0, FIRST)
                    old["out"]()
                    old["out_lo"]()
                loop("dve", 1, nh, body)
                old = scan(nh - 1)
                old["diffs"](FIRST, LV - 1)
                for part in ("decayed", "products", "levels", "states", "out", "out_lo"):
                    old[part]()
                dve.wait_ge(S["sp_stored"], 16 * (g0 + nh + 1))
                dve.wait_ge(S["ss_stored"], 16 * (g0 + nh + 1))

            dve.wait_ge(S["rs_ready"], 2)
            states_out(dve)
            dve.sem_inc(S["head_out"], 1)
            heads("ab_heads", 4, GM, 0, V_GN, 1)

            def gate(m, ps, b):
                TT(two(GG[:, :]), pair(ps), two(RS[:, :]), ALU.mult).then_inc(S["g_scaled"], 1)
                dve.drain().then_inc(S["pair_read"], 1)
                hold("dve", S["gs_ready"], m + 1)
                TT(GG[:, :], GS[:, :], tile(ON, m), ALU.mult).then_inc(S["go_made"], 1)
                dve.drain()
                hold("dve", S["goh_ready"], m + 1)
                TT(tile(GOL, m), GG[:, :], tile(GOH, m).bitcast(F), ALU.subtract)
                dve.drain().then_inc(S["gol_ready"], 1)
            run("ab_g", gate)
            clear_acc()
            run("ab_outo", residual(2, 1.0, True))
            ffn("l0f2", 3)
            ffn("l1f1", 4)
            dve.wait_ge(S["rs_ready"], 5)
            heads("c_heads", 8, CM, 4, V_HN, 2)
            clear_acc()
            run("c_out", residual(5, 1.0, True))
            ffn("l1f2", 6, final=True)
            dve.wait_ge(S["rs_ready"], 7)
            dve.memset(YF[:, :, T:TPAD], 0.0)
            for m in range(KT):
                STT(YF[:, m, 0:T], H[:, m, :], vec[:, V_FIN + m:V_FIN + m + 1], RS[:, :], ALU.mult, ALU.mult)
            dve.drain().then_inc(S["y_ready"], 1)

        @block.tensor
        def _(pe):
            mm = pe.matmul

            def unit(ps, i, k, rh, rl, before=None):
                hold("pe", S["lo_ready"], 2 * i + (ps + 1 + CREDIT))
                hold("pe", S["pair_read"], 2 * i + (ps - 1 + CREDIT))
                for p, (wt, x) in enumerate(((whi, rh), (whi, rl), (wlo, rh))):
                    for r in range(k):
                        if before:
                            before(p, r)
                        for s in range(2):
                            last = mm(PD[:, 2 * (ps % 2) + s, 0:HT], wt[ps % 2][:, r, :], x[:, r, s * HT:(s + 1) * HT],
                                      start=(p == 0 and r == 0), stop=(p == 2 and r == k - 1))
                last.then_inc(S["unit_done"], 1)

            def run(name, rh, rl, before=None, after_first=None):
                u0, n, k = plan[name]
                unit(u0, 0, k, rh, rl, before)
                if after_first:
                    after_first()
                if n > 1:
                    unit(u0 + 1, 0, k, rh, rl)
                    run_rest(name, rh, rl)

            def run_rest(name, rh, rl):
                u0, n, k = plan[name]
                loop("pe", 1, n // 2, lambda i: (unit(u0, i, k, rh, rl), unit(u0 + 1, i, k, rh, rl)))

            def unit_rows(ps, r0, r1, k, rh, rl):
                if r0 == 0:
                    pe.wait_ge(S["lo_ready"], ps + 1 + CREDIT)
                    pe.wait_ge(S["pair_read"], ps - 1 + CREDIT)
                for r in range(r0, r1):
                    for p, (wt, x) in enumerate(((whi, rh), (whi, rl), (wlo, rh))):
                        for s in range(2):
                            last = mm(PD[:, 2 * (ps % 2) + s, 0:HT], wt[ps % 2][:, r, :], x[:, r, s * HT:(s + 1) * HT],
                                      start=(p == 0 and r == 0), stop=(p == 2 and r == k - 1))
                if r1 == k:
                    last.then_inc(S["unit_done"], 1)

            def parts_of(hs, ls, hbase, lbase):
                def before(p, r):
                    if p < 2:
                        pe.wait_ge((hs, ls)[p], (hbase, lbase)[p] + r + 1)
                return before

            def mean_square(e):
                pe.wait_ge(S["acc_done"], 9 * e + 9)
                for s in range(2):
                    last = mm(PM[:, s, 0:HT], ones[:, :], ACC[:, s * HT:(s + 1) * HT], start=True, stop=True)
                last.then_inc(S["ms_ready"], 1)

            def x_parts(e):
                return parts_of(S["xh_ready"], S["xl_ready"], e * KT, e * KT)

            hidden = [0]

            def ffn(tag, e):
                for g, (_, nf) in enumerate(GROUPS):
                    if g == 0:
                        run(f"{tag}_up{g}", XH, XL, x_parts(e), lambda: mean_square(e))
                    else:
                        run(f"{tag}_up{g}", XH, XL)
                    run(f"{tag}_down{g}", AH, AL, parts_of(S["ah_ready"], S["al_ready"], hidden[0], hidden[0]))
                    hidden[0] += nf

            pe.sem_inc(S["unit_done"], CREDIT)
            pe.wait_ge(S["consts_made"], 2)
            pe.wait_ge(S["rows_landed"], 16 * 12)
            for n in range(3):
                last = pe.transpose(PM[:, 2, n * P:(n + 1) * P], rows[:, n, :], ident[:, :])
            last.then_inc(S["vec_psum"], 1)
            pe.wait_ge(S["vec_ready"], 1)
            pe.wait_ge(x_landed[0], 16)
            pe.wait_ge(x_landed[1], 16)
            for m in range(KT):
                if m >= 2:
                    pe.wait_ge(S["h_ready"], m - 1)
                b = 2 * (m % 2)
                for c in range(NC):
                    pe.transpose(PM[:, b, c * P:(c + 1) * P], xin[:, c, m * P:(m + 1) * P], ident[:, :])
                mm(PM[:, b + 1, 0:TS], xin[0:TS, NC, m * P:(m + 1) * P], ident[0:TS, 0:TS], start=True, stop=True).then_inc(S["x_psum"], 1)
            ffn("l0f1", 0)

            run("ab_small", XH, XL, x_parts(1), lambda: mean_square(1))
            run("ab_xbc", XH, XL)

            def turn_state(src, bank, signal):
                for m in range(KT):
                    last = pe.transpose(PM[:, bank + m // 4, (m % 4) * P:(m % 4 + 1) * P], src(m), ident[:, :])
                last.then_inc(S[signal], 1)

            def ssd_inputs():
                pe.wait_ge(S["last_rows"], 1)
                pe.transpose(PM[:, 2, 0:P], XLAST[:, :], ident[:, :]).then_inc(S["last_psum"], 1)
                pe.wait_ge(S["selectors"], 1)
                pe.wait_ge(S["small_landed"], 64)
                for m in range(KT):
                    last = mm(PM[:, 3, m:m + 1], SELP[32:48, m, :], D16[32:48, 0:1], start=True, stop=True)
                last.then_inc(S["d_psum"], 1)
                pe.wait_ge(S["rs_ready"], 2)
                pe.wait_ge(S["h0_landed"], 32)
                turn_state(lambda m: H0[:, m, :], 0, "h0_psum")
            run("ab_z", XH, XL, after_first=ssd_inputs)

            def chunk(c, n, state=HS):
                hold("pe", S["chunk_copied"], c + 1)
                for m in range(KT):
                    pe.transpose(PM[:, m // 4, (m % 4) * P:(m % 4 + 1) * P], XCC[:, m, :], ident[:, :])
                for g in range(2):
                    pe.transpose(PM[:, 2, g * P:(g + 1) * P], XCC[:, KT + g, :], ident[:, :])
                pe.transpose(PM[:, 2, 2 * P:3 * P], DCC[:, :], ident[:, :]).then_inc(S["chunk_turned"], 1)
                for h in range(HA):
                    last = mm(PD[:, h // 4, (h % 4) * CH:(h % 4 + 1) * CH], SEL[0:64, h, :], DCC[0:64, :], start=True, stop=True)
                    if h % 4 == 3:
                        last.then_inc(S["cum_psum"], 1)
                hold("pe", S["chunk_dct"], c + 1)
                mm(PM[:, 2, 384:384 + HA], ones[32:48, :], CE[32:48, :], start=True, stop=True).then_inc(S["end_psum"], 1)
                hold("pe", S["y_rstd"], c + 1)
                for g in range(2):
                    last = mm(PM[:, 3, g * CH:(g + 1) * CH], XCC[:, KT + g, :], XCC[:, KT + 2 + g, :], start=True, stop=True)
                last.then_inc(S["cb_psum"], 1)
                hold("pe", S["x_scaled"], c + 1)
                for m in range(KT):
                    last = mm(PM[:, m // 4, (m % 4) * CH:(m % 4 + 1) * CH], SELP[0:64, m, :], DCC[0:64, :], start=True, stop=True)
                last.then_inc(S["spread_psum"], 1)
                hold("pe", S["decay_exp"], 4 * c + 4)
                for m in range(KT):
                    mm(PD[:, 2 + m // 4, (m % 4) * CH:(m % 4 + 1) * CH], state[:, m * P:(m + 1) * P], XCC[:, KT + 2 + m // 4, :], start=True, stop=True)
                for h in range(HA):
                    if h % 4 == 0:
                        hold("pe", S["decay_made"], 4 * c + (h // 4 + 1))
                    m, e = h // 2, h % 2
                    last = mm(PD[e * PA:(e + 1) * PA, m // 4, (m % 4) * CH:(m % 4 + 1) * CH], XD[:, h * PA:(h + 1) * PA],
                              LM[:, h // 4, h % 4, :], start=True, stop=True)
                last.then_inc(S["y_psum"], 1)
                hold("pe", S["spread_exp"], c + 1)
                for g in range(2):
                    last = mm(PM[:, g, :], BT[0:n, g * P:(g + 1) * P], XDE[0:n, g * 512:(g + 1) * 512], start=True, stop=True)
                last.then_inc(S["state_psum"], 1)
                hold("pe", S["y_squared"], c + 1)
                for g in range(2):
                    for m in range(4):
                        last = mm(PM[:, 3, (2 + g) * CH:(3 + g) * CH], ones[:, :], EP[:, 4 * g + m, :], start=(m == 0), stop=(m == 3))
                last.then_inc(S["y_mean"], 1)

            pe.wait_ge(S["pair_read"], plan["ab_outy"][0] + CREDIT)
            pe.wait_ge(S["h0_ready"], 1)
            with pe.Fori(0, NC) as c:
                chunk(c, CH)
            chunk(NC, TS, HSS)
            pe.wait_ge(S["state_new"], NC + 2)
            turn_state(lambda m: HS[:, m * P:(m + 1) * P], 0, "hout_psum")
            pe.wait_ge(S["yh_ready"], NC + 1)
            pe.wait_ge(S["yl_ready"], NC + 2)
            run("ab_outy", YH, YL, after_first=lambda: turn_state(lambda m: HSS[:, m * P:(m + 1) * P], 2, "hout_psum"))

            def heads(name, nh, m, g0, t0, ahead, before=None, after_first=None):
                u0 = plan[name][0]
                nv = m["nv"]
                gla = nv == 2
                vt, kt, att, ats, s, si, qe = (m[x] for x in ("vt", "kt", "att", "ats", "s", "si", "qe"))

                def scan(j):
                    g = j + g0

                    def logits():
                        if gla:
                            hold("pe", S["wg_copied"], j + 1)
                            if not isinstance(j, int):
                                hold("pe", S["o_copied"], g)
                            for e in range(2):
                                last = mm(PM[:, e, 0:HT], m["wg"][32:48, :], DTG[32:48, e * HT:(e + 1) * HT], start=True, stop=True)
                            last.then_inc(S["gk_psum"], 1)

                    def turn():
                        hold("pe", S["pre_act"], g + 1)
                        for v in range(nv + 1):
                            if v == nv:
                                hold("pe", S["kd_ready"], g + 1)
                            elif v == 1:
                                hold("pe", S["last_taken"], g + 1)
                            if v >= 2:
                                hold("pe", S["turned_read"], (nv + 1) * j + (t0 + v - 1))
                            src, b = (m["vw"][:, v, :] if v < nv else m["kd"][:, :]), 2 * (v % 2)
                            for c in range(NC):
                                pe.transpose(PM[:, b, c * P:(c + 1) * P], src[:, c * CH:(c + 1) * CH], ident[:, :])
                            pe.transpose(PM[:, b + 1, 0:P], src[:, TP:TPAD], ident[:, :]).then_inc(S["turned"], 1)

                    def tree():
                        hold("pe", S["turned_read"], (nv + 1) * j + (t0 + nv + 1))
                        for n in range(LV):
                            hf = TREE[n] if n < LV - 1 else 0
                            if n < LV - 1:
                                hold("pe", S["tree_made"], (LV - 1) * g + (n + 1))
                            if n >= 2:
                                hold("pe", S["level_placed"], LV * g + (n - 1))
                            if n < 2:
                                for k in range(TP // (2 * hf)):
                                    t = 2 * hf * k
                                    p = t % CH
                                    last = mm(PM[p:p + hf, n % 2, t + hf:t + 2 * hf], m["xl"][:, n, t:t + hf], m["xl"][:, n, t + hf:t + 2 * hf],
                                              start=True, stop=True)
                            else:
                                l, r = (m["xl"][:, n, :], m["xl"][:, n, :]) if hf else (m["kw"][:, :], m["qw"][:, :])
                                for c in range(NC):
                                    mm(PM[:, n % 2, c * CH:(c + 1) * CH], l[:, c * CH:(c + 1) * CH], r[:, c * CH:(c + 1) * CH], start=True, stop=True)
                                last = mm(PM[0:TS, 2 + n % 2, 0:TS], l[:, TP:T], r[:, TP:T], start=True, stop=True)
                            last.then_inc(S["level_psum"], 1)

                    def outputs():
                        hold("pe", S["level_placed"], LV * g + LV)
                        per = 4 // nv
                        for c in range(NC + 1):
                            last = mm(PM[:, c // per, (c % per) * nv * P:(c % per + 1) * nv * P], kt[:, c, :], vt[:, c, :], start=True, stop=True)
                        last.then_inc(S["kv_psum"], 1)
                        hold("pe", S["s_ready"], g + 1)
                        for v in range(nv):
                            vs = slice(v * P, (v + 1) * P)
                            for c in range(NC):
                                cs = slice(c * CH, (c + 1) * CH)
                                mm(PM[:, v, cs], vt[:, c, vs], att[:, c, :], start=True, stop=(c == 0))
                                if c:
                                    mm(PM[:, v, cs], s[:, c - 1, vs], qe[:, cs], start=False, stop=True)
                            mm(PM[:, 2, v * TS:(v + 1) * TS], vt[0:TS, NC, vs], ats[0:TS, :], start=True, stop=False)
                            last = mm(PM[:, 2, v * TS:(v + 1) * TS], si[:, vs], qe[:, TP:T], start=False, stop=True)
                        last.then_inc(S["o_psum"], 1)

                    def squares():
                        hold("pe", S["o_copied"], g + 1)
                        for e in range(2):
                            for v in range(nv):
                                last = mm(PM[:, 2 + e, 0:HT], ones[:, :], m["sq"][:, v, e * HT:(e + 1) * HT], start=(v == 0), stop=(v == nv - 1))
                        last.then_inc(S["o_mean"], 1)
                    return logits, turn, tree, outputs, squares

                for b in range(4):
                    unit(u0 + b, 0, KT, XH, XL, before if b == 0 else None)
                    if b == 0 and after_first:
                        after_first()

                scan(0)[0]()

                def body(h):
                    _, turn, tree, outputs, squares = scan(h - 1)
                    unit(u0, 2 * h, KT, XH, XL)
                    unit(u0 + 1, 2 * h, KT, XH, XL)
                    unit(u0 + 2, 2 * h, KT, XH, XL)
                    turn()
                    tree()
                    outputs()
                    unit(u0 + 3, 2 * h, KT, XH, XL)
                    scan(h)[0]()
                    squares()
                loop("pe", 1, nh, body)
                ahead()
                for part in scan(nh - 1)[1:]:
                    part()

            def first_gates():
                for b in range(2):
                    unit(plan["ab_g"][0] + b, 0, KT, XH, XL)
            heads("ab_heads", 4, GM, 0, 0, first_gates)
            run_rest("ab_g", XH, XL)
            run("ab_outo", GOH, GOL, parts_of(S["goh_ready"], S["gol_ready"], 0, 0))
            ffn("l0f2", 2)
            ffn("l1f1", 3)

            def first_outs():
                pe.wait_ge(S["head_out"], 12)
                for b in range(2):
                    unit_rows(plan["c_out"][0] + b, 0, KT - 1, KT, COH, COL)
            heads("c_heads", 8, CM, 4, 12, first_outs, x_parts(4), lambda: (mean_square(4), pe.wait_ge(S["rs_ready"], 5)))
            pe.wait_ge(S["head_out"], 13)
            for b in range(2):
                unit_rows(plan["c_out"][0] + b, KT - 1, KT, KT, COH, COL)
            run_rest("c_out", COH, COL)
            ffn("l1f2", 5)
            mean_square(6)
            pe.wait_ge(S["y_ready"], 1)
            for c in range(NC + 1):
                if c >= 2:
                    pe.wait_ge(S["yt_copied"], c - 1)
                b = 2 * (c % 2)
                for m in range(KT):
                    last = pe.transpose(PM[:, b + m // 4, (m % 4) * P:(m % 4 + 1) * P], YF[:, m, c * CH:(c + 1) * CH], ident[:, :])
                last.then_inc(S["yt_psum"], 1)


INPUTS = ["x_prompt", "x_sample", "state_ssm", "state_conv", "state_gla", "state_hgrn", "norm_ffn1", "ffn1_w_gu",
          "ffn1_w_down", "norm_mix", "ab_w_in", "ssm_conv_w", "ssm_conv_b", "ssm_dt_bias", "ssm_a_log", "ssm_d",
          "ssm_norm_w", "gla_w_gk", "gla_b_gk", "gla_norm_w", "ab_w_out", "c_w_in", "hgrn_lb_logits", "hgrn_norm_w",
          "c_w_out", "norm_ffn2", "ffn2_w_gu", "ffn2_w_down", "norm_final"]
OUTPUTS = [("y_p", (1, 512, 1024)), ("y_s", (1, 32, 1024)),
           ("ssm_p", (1, 1, 16, 64, 128)), ("conv_p", (1, 1, 3, 1536)), ("gla_p", (1, 1, 4, 128, 256)), ("hgrn_p", (1, 1, 8, 128, 128)),
           ("ssm_s", (1, 1, 16, 64, 128)), ("conv_s", (1, 1, 3, 1536)), ("gla_s", (1, 1, 4, 128, 256)), ("hgrn_s", (1, 1, 8, 128, 128))]


def kernel(**inputs):
    import numpy as np
    import concourse.bacc as bacc
    from concourse.bass_utils import run_bass_kernel_spmd

    nc = bacc.Bacc("TRN2", target_bir_lowering=False, num_devices=1)
    arrays, a, o = {}, {}, {}
    for name in INPUTS:
        x = np.ascontiguousarray(inputs[name])
        arrays["in_" + name] = x
        a[name] = nc.dram_tensor("in_" + name, x.shape, F, kind="ExternalInput").ap()
    for name, shape in OUTPUTS:
        o[name] = nc.dram_tensor("out_" + name, shape, F, kind="ExternalOutput").ap()
    build(nc, a, o)
    r = run_bass_kernel_spmd(nc, [arrays], core_ids=[0])
    return tuple(r.results[0]["out_" + name] for name, _ in OUTPUTS)
```
